# Optimizing a Trainium2 kernel written in Bass

```python
import jax, jax.numpy as jnp
from jax import lax
import numpy as np
import math

D_MODEL = 2048
BATCH = 1
SEQ = 256
DEPTH = 2

MEM_TOKENS = 256
EPS = 1e-6
ROPE_THETA = 10000.0
Q_BLOCK = 128
MLA_HEADS = D_MODEL // 256
QK_NOPE_DIM = 128
QK_ROPE_DIM = 64
QK_HEAD_DIM = QK_NOPE_DIM + QK_ROPE_DIM
V_HEAD_DIM = 128
Q_LORA_RANK = D_MODEL // 4
KV_LORA_RANK = D_MODEL // 8
MLA_WIDTH = MLA_HEADS * V_HEAD_DIM
CONV_WIDTH = D_MODEL // 4
CONV_K = 3
MEM_HEADS = 4
MEM_HEAD_DIM = D_MODEL // 16
MEM_WIDTH = MEM_HEADS * MEM_HEAD_DIM
MIX_WIDTH = MLA_WIDTH + CONV_WIDTH + MEM_WIDTH
IN_SPLITS = (Q_LORA_RANK, KV_LORA_RANK, QK_ROPE_DIM, CONV_WIDTH, CONV_WIDTH, CONV_WIDTH, MEM_WIDTH, MIX_WIDTH)
IN_COLS = Q_LORA_RANK + KV_LORA_RANK + QK_ROPE_DIM + 3 * CONV_WIDTH + MEM_WIDTH + MIX_WIDTH


def rmsnorm(x, g):
    x32 = x.astype(jnp.float32)
    y = x32 * lax.rsqrt(jnp.mean(x32 * x32, axis=-1, keepdims=True) + EPS)
    return (y * g.astype(jnp.float32)).astype(x.dtype)

def rope_tables(positions):
    inv_freq = 1.0 / (ROPE_THETA ** (jnp.arange(0, QK_ROPE_DIM, 2, dtype=jnp.float32) / QK_ROPE_DIM))
    ang = positions.astype(jnp.float32)[..., None] * inv_freq
    return jnp.cos(ang), jnp.sin(ang)

def apply_rope(x, cos, sin):
    half = x.shape[-1] // 2
    x32 = x.astype(jnp.float32)
    x1, x2 = x32[..., :half], x32[..., half:]
    return jnp.concatenate([x1 * cos - x2 * sin, x2 * cos + x1 * sin], axis=-1).astype(x.dtype)

def split_cols(z):
    idx = list(np.cumsum(IN_SPLITS)[:-1])
    return jnp.split(z, idx, axis=-1)

def mla_attention(q, k, v):
    b, s, h, dq = q.shape
    nb = s // Q_BLOCK
    scale = QK_HEAD_DIM ** -0.5
    qb = q.reshape(b, nb, Q_BLOCK, h, dq).transpose(1, 0, 2, 3, 4)

    def block(qi):
        sc = jnp.einsum('bqhd,bkhd->bhqk', qi, k).astype(jnp.float32) * scale
        p = jax.nn.softmax(sc, axis=-1).astype(v.dtype)
        return jnp.einsum('bhqk,bkhd->bqhd', p, v)

    o = lax.map(block, qb)
    return o.transpose(1, 0, 2, 3, 4).reshape(b, s, h * V_HEAD_DIM)

def short_gated_conv(gb, gc, xin, w):
    u = gc * xin
    up = jnp.pad(u, ((0, 0), (1, 1), (0, 0)))
    conv = up[:, :-2] * w[0] + up[:, 1:-1] * w[1] + up[:, 2:] * w[2]
    return gb * conv

def memory_attention(q, mem_n, w_mk, w_mv):
    b, m, _ = mem_n.shape
    mk = (mem_n @ w_mk).reshape(b, m, MEM_HEADS, MEM_HEAD_DIM)
    mv = (mem_n @ w_mv).reshape(b, m, MEM_HEADS, MEM_HEAD_DIM)
    sc = jnp.einsum('bshd,bmhd->bhsm', q, mk).astype(jnp.float32) * (MEM_HEAD_DIM ** -0.5)
    p = jax.nn.softmax(sc, axis=-1).astype(mv.dtype)
    o = jnp.einsum('bhsm,bmhd->bshd', p, mv)
    return o.reshape(b, q.shape[1], MEM_WIDTH)

def first_inputs(seed: int = 0) -> dict:
    key = jax.random.key(seed)
    ks = jax.random.split(key, 16)
    f32 = jnp.float32

    def w(k, shape, fan_in):
        return jax.random.normal(k, shape, f32) * (fan_in ** -0.5)

    def gain(k, shape):
        return 1.0 + 0.02 * jax.random.normal(k, shape, f32)

    x = jax.random.normal(ks[0], (BATCH, SEQ, D_MODEL), f32)
    mem = jax.random.normal(ks[1], (BATCH, MEM_TOKENS, D_MODEL), f32)
    offset = jax.random.randint(ks[2], (BATCH, 1), 0, 4096, dtype=jnp.int32)
    positions = (offset + jnp.arange(SEQ, dtype=jnp.int32)[None, :]).astype(jnp.int32)
    return {
        "x": x,
        "mem": mem,
        "positions": positions,
        "pre_norm_g": gain(ks[3], (DEPTH, D_MODEL)),
        "w_in": w(ks[4], (DEPTH, D_MODEL, IN_COLS), D_MODEL),
        "q_norm_g": gain(ks[5], (DEPTH, Q_LORA_RANK)),
        "w_uq": w(ks[6], (DEPTH, Q_LORA_RANK, MLA_HEADS * QK_HEAD_DIM), Q_LORA_RANK),
        "kv_norm_g": gain(ks[7], (DEPTH, KV_LORA_RANK)),
        "w_ukv": w(ks[8], (DEPTH, KV_LORA_RANK, MLA_HEADS * (QK_NOPE_DIM + V_HEAD_DIM)), KV_LORA_RANK),
        "conv_w": w(ks[9], (DEPTH, CONV_K, CONV_WIDTH), CONV_K),
        "mem_norm_g": gain(ks[10], (DEPTH, D_MODEL)),
        "w_mk": w(ks[11], (DEPTH, D_MODEL, MEM_WIDTH), D_MODEL),
        "w_mv": w(ks[12], (DEPTH, D_MODEL, MEM_WIDTH), D_MODEL),
        "w_o": w(ks[13], (DEPTH, MIX_WIDTH, D_MODEL), MIX_WIDTH),
        "post_norm_g": gain(ks[14], (DEPTH, D_MODEL)),
    }

def first_block(x, mem, positions, pre_norm_g, w_in, q_norm_g, w_uq, kv_norm_g, w_ukv, conv_w,
              mem_norm_g, w_mk, w_mv, w_o, post_norm_g):
    b, s, _ = x.shape
    cos, sin = rope_tables(positions)
    for l in range(DEPTH):
        h = rmsnorm(x, pre_norm_g[l])
        z = h @ w_in[l]
        q_lat, kv_lat, k_pe, gb, gc, xin, q_mem, gate = split_cols(z)

        q = (rmsnorm(q_lat, q_norm_g[l]) @ w_uq[l]).reshape(b, s, MLA_HEADS, QK_HEAD_DIM)
        q = jnp.concatenate([q[..., :QK_NOPE_DIM],
                             apply_rope(q[..., QK_NOPE_DIM:], cos[:, :, None, :], sin[:, :, None, :])], axis=-1)
        kv = (rmsnorm(kv_lat, kv_norm_g[l]) @ w_ukv[l]).reshape(b, s, MLA_HEADS, QK_NOPE_DIM + V_HEAD_DIM)
        k_nope, v = kv[..., :QK_NOPE_DIM], kv[..., QK_NOPE_DIM:]
        k_pe = apply_rope(k_pe, cos, sin)
        k = jnp.concatenate([k_nope, jnp.broadcast_to(k_pe[:, :, None, :], (b, s, MLA_HEADS, QK_ROPE_DIM))], axis=-1)
        a_out = mla_attention(q, k, v)

        c_out = short_gated_conv(gb, gc, xin, conv_w[l])

        mem_n = rmsnorm(mem, mem_norm_g[l])
        m_out = memory_attention(q_mem.reshape(b, s, MEM_HEADS, MEM_HEAD_DIM), mem_n, w_mk[l], w_mv[l])

        y = jnp.concatenate([a_out, c_out, m_out], axis=-1) * jax.nn.silu(gate)
        o = y @ w_o[l]
        x = x + rmsnorm(o, post_norm_g[l])
    return x


DEPTH_2 = 1

GRID_W = 64
CTX_LEN = 256
N_MIXERS = 3
N_MOD = 6
MLP_HIDDEN = 4 * D_MODEL
NORM_EPS = 1e-6
FNET_GROUPS = 8
FNET_GROUP_DIM = D_MODEL // FNET_GROUPS
HGRN_EXPAND = 128
HGRN_HEADS = D_MODEL // HGRN_EXPAND
HGRN_DK = HGRN_EXPAND
HGRN_DV = D_MODEL // HGRN_HEADS
HGRN_F = HGRN_HEADS * HGRN_DK
HGRN_CHUNK = 16
DIFF_HEAD_DIM = 128
DIFF_HEADS = D_MODEL // (2 * DIFF_HEAD_DIM)
DIFF_V_DIM = 2 * DIFF_HEAD_DIM
ROPE_BASE = 10000.0


F32 = jnp.float32

def rms_norm(x, g):
    xf = x.astype(F32)
    y = xf * lax.rsqrt(jnp.mean(xf * xf, axis=-1, keepdims=True) + NORM_EPS)
    return (y * g.astype(F32)).astype(x.dtype)

def modulate(h, shift, scale):
    return h * (1 + scale) + shift

def sqrelu_mlp(h, w1, w2):
    return jnp.square(jax.nn.relu(h @ w1)) @ w2

def axial_rope_tables(n_tokens, dim):
    rows = n_tokens // GRID_W
    row = jnp.broadcast_to(jnp.arange(rows)[:, None], (rows, GRID_W)).reshape(-1).astype(F32)
    col = jnp.broadcast_to(jnp.arange(GRID_W)[None, :], (rows, GRID_W)).reshape(-1).astype(F32)
    n_freq = dim // 4
    inv = ROPE_BASE ** (-jnp.arange(n_freq, dtype=F32) / n_freq)
    ang = jnp.concatenate([row[:, None] * inv, col[:, None] * inv], axis=-1)
    return jnp.cos(ang), jnp.sin(ang)

def apply_rope_2(x, cos, sin):
    xf = x.astype(F32)
    x1, x2 = jnp.split(xf, 2, axis=-1)
    return jnp.concatenate([x1 * cos - x2 * sin, x1 * sin + x2 * cos], axis=-1).astype(x.dtype)

def fourier_mix(h):
    B, L, D = h.shape
    hg = h.astype(F32).reshape(B, L, FNET_GROUPS, FNET_GROUP_DIM)
    return jnp.fft.fftn(hg, axes=(1, 3)).real.reshape(B, L, D).astype(h.dtype)

def hgrn_lower_bounds(p):
    cs = jnp.cumsum(jax.nn.softmax(p.astype(F32), axis=0), axis=0)
    return cs - cs[0:1]

def chunk_gla(q, k, v, logf, s0):
    B, H, L, dk = q.shape
    C = HGRN_CHUNK
    N = L // C
    r = lambda t: jnp.moveaxis(t.astype(F32).reshape(B, H, N, C, t.shape[-1]), 2, 0)
    bcum = jnp.cumsum(logf.astype(F32).reshape(B, H, N, C, dk), axis=3)
    xs = (r(q), r(k), r(v), jnp.moveaxis(bcum, 2, 0))
    mask = jnp.tril(jnp.ones((C, C), dtype=bool))[:, :, None]

    def step(s, inp):
        qc, kc, vc, bc = inp
        bl = bc[:, :, -1:, :]
        decay = jnp.exp(jnp.where(mask, bc[:, :, :, None, :] - bc[:, :, None, :, :], -jnp.inf))
        a = jnp.einsum('bhtd,bhsd,bhtsd->bhts', qc, kc, decay)
        o = jnp.einsum('bhts,bhsv->bhtv', a, vc) + jnp.einsum('bhtd,bhdv->bhtv', qc * jnp.exp(bc), s)
        s = jnp.exp(bl[:, :, 0, :])[..., None] * s + jnp.einsum('bhsd,bhsv->bhdv', kc * jnp.exp(bl - bc), vc)
        return s, o

    s_final, o = lax.scan(step, s0.astype(F32), xs)
    return jnp.moveaxis(o, 0, 2).reshape(B, H, L, v.shape[-1]), s_final

def hgrn2_mixer(h_lat, h_ctx, w_in, lb, gnorm, w_out, ctx_out):
    lb = lb.reshape(2, HGRN_HEADS, HGRN_DK)

    def project(h):
        B, L, _ = h.shape
        q, zf, zb, v, g = jnp.split(h @ w_in, [HGRN_F, 2 * HGRN_F, 3 * HGRN_F, 3 * HGRN_F + D_MODEL], axis=-1)
        hd = lambda t: t.reshape(B, L, HGRN_HEADS, -1).transpose(0, 2, 1, 3)
        return hd(q), hd(zf), hd(zb), hd(v), hd(g)

    def forget(z, lbd):
        zf = z.astype(F32)
        l = lbd[None, :, None, :]
        logf = jnp.logaddexp(jnp.log(l), jnp.log1p(-l) + jax.nn.log_sigmoid(zf))
        key = (1 - l) * jax.nn.sigmoid(-zf)
        return logf, key

    def readout(o, g, dtype):
        B, H, L, _ = o.shape
        y = rms_norm(o, gnorm) * jax.nn.silu(g.astype(F32))
        return y.transpose(0, 2, 1, 3).reshape(B, L, H * HGRN_DV).astype(dtype) @ w_out

    flip = lambda t: jnp.flip(t, axis=2)
    qc, zfc, zbc, vc, gc = project(h_ctx)
    ql, zfl, zbl, vl, gl = project(h_lat)
    s0 = jnp.zeros((qc.shape[0], HGRN_HEADS, HGRN_DK, HGRN_DV), F32)
    lfc, kfc = forget(zfc, lb[0])
    o_cf, s_f = chunk_gla(qc, kfc, vc, lfc, s0)
    lfl, kfl = forget(zfl, lb[0])
    o_lf, _ = chunk_gla(ql, kfl, vl, lfl, s_f)
    lbc, kbc = forget(zbc, lb[1])
    o_cb, s_b = chunk_gla(flip(qc), flip(kbc), flip(vc), flip(lbc), s0)
    lbl, kbl = forget(zbl, lb[1])
    o_lb, _ = chunk_gla(flip(ql), flip(kbl), flip(vl), flip(lbl), s_b)
    y_lat = readout(o_lf + flip(o_lb), gl, h_lat.dtype)
    y_ctx = readout(o_cf + flip(o_cb), gc, h_ctx.dtype) if ctx_out else None
    return y_lat, y_ctx

def diff_core(q, k, v, lam):
    s = jnp.einsum('bhmqd,bhmkd->bhmqk', q, k).astype(F32) * (DIFF_HEAD_DIM ** -0.5)
    p = jax.nn.softmax(s, axis=-1)
    a = p[:, :, 0] - lam * p[:, :, 1]
    return jnp.einsum('bhqk,bhkv->bhqv', a.astype(v.dtype), v)

def diff_attention(h_lat, h_ctx, w_qkv, lam_p, subln, w_out, lambda_init, cos, sin, ctx_out):
    def project(h):
        B, L, _ = h.shape
        q, k, v = jnp.split(h @ w_qkv, 3, axis=-1)
        q = q.reshape(B, L, DIFF_HEADS, 2, DIFF_HEAD_DIM).transpose(0, 2, 3, 1, 4)
        k = k.reshape(B, L, DIFF_HEADS, 2, DIFF_HEAD_DIM).transpose(0, 2, 3, 1, 4)
        v = v.reshape(B, L, DIFF_HEADS, DIFF_V_DIM).transpose(0, 2, 1, 3)
        return q, k, v

    def merge(o, dtype):
        B, H, L, _ = o.shape
        o = rms_norm(o, subln) * (1 - lambda_init)
        return o.transpose(0, 2, 1, 3).reshape(B, L, H * DIFF_V_DIM).astype(dtype) @ w_out

    lp = lam_p.astype(F32)
    lam = jnp.exp(jnp.sum(lp[0] * lp[1])) - jnp.exp(jnp.sum(lp[2] * lp[3])) + lambda_init
    q_c, k_c, v_c = project(h_ctx)
    q_l, k_l, v_l = project(h_lat)
    q_l, k_l = apply_rope_2(q_l, cos, sin), apply_rope_2(k_l, cos, sin)
    k_all = jnp.concatenate([k_c, k_l], axis=3)
    v_all = jnp.concatenate([v_c, v_l], axis=2)
    B, H, _, L, d = q_l.shape
    nb = L // Q_BLOCK
    q_blocks = jnp.moveaxis(q_l.reshape(B, H, 2, nb, Q_BLOCK, d), 3, 0)
    o_blocks = lax.map(lambda qb: diff_core(qb, k_all, v_all, lam), q_blocks)
    o_l = jnp.moveaxis(o_blocks, 0, 2).reshape(B, H, L, DIFF_V_DIM)
    y_lat = merge(o_l, h_lat.dtype)
    y_ctx = merge(diff_core(q_c, k_c, v_c, lam), h_ctx.dtype) if ctx_out else None
    return y_lat, y_ctx

def second_inputs(seed: int = 0) -> dict:
    key = jax.random.key(seed)
    ks = jax.random.split(key, 20)
    n_slot = lambda m: len(range(m, DEPTH_2, N_MIXERS))
    n_a, n_b, n_c = n_slot(0), n_slot(1), n_slot(2)
    D = D_MODEL
    nrm = lambda k, shape, s: jax.random.normal(k, shape, F32) * s
    return {
        'x': nrm(ks[0], (BATCH, SEQ, D), 1.0),
        'c': nrm(ks[1], (BATCH, D), 1.0),
        'ctx': nrm(ks[2], (BATCH, CTX_LEN, D), 1.0),
        'c_ctx': nrm(ks[3], (D,), 1.0),
        'w_mod': nrm(ks[4], (DEPTH_2, D, N_MOD * D), D ** -0.5),
        'b_mod': nrm(ks[5], (DEPTH_2, N_MOD * D), 0.01),
        'norm_g': 1.0 + nrm(ks[6], (DEPTH_2, 4, D), 0.02),
        'w_mlp_in': nrm(ks[7], (DEPTH_2, D, MLP_HIDDEN), D ** -0.5),
        'w_mlp_out': nrm(ks[8], (DEPTH_2, MLP_HIDDEN, D), MLP_HIDDEN ** -0.5),
        'fnet_w_out': nrm(ks[9], (n_a, D, D), D ** -0.5),
        'hgrn_w_in': nrm(ks[10], (n_b, D, 3 * HGRN_F + 2 * D), D ** -0.5),
        'hgrn_lb': nrm(ks[11], (DEPTH_2, 2, HGRN_F), 0.1),
        'hgrn_gnorm': 1.0 + nrm(ks[12], (n_b, HGRN_DV), 0.02),
        'hgrn_w_out': nrm(ks[13], (n_b, D, D), D ** -0.5),
        'diff_w_qkv': nrm(ks[14], (n_c, D, 3 * D), D ** -0.5),
        'diff_lambda': nrm(ks[15], (n_c, 4, DIFF_HEAD_DIM), 0.1),
        'diff_subln': 1.0 + nrm(ks[16], (n_c, DIFF_V_DIM), 0.02),
        'diff_w_out': nrm(ks[17], (n_c, D, D), D ** -0.5),
    }

def second_block(x, c, ctx, c_ctx, w_mod, b_mod, norm_g, w_mlp_in, w_mlp_out, fnet_w_out, hgrn_w_in, hgrn_lb, hgrn_gnorm, hgrn_w_out, diff_w_qkv, diff_lambda, diff_subln, diff_w_out):
    L = x.shape[1]
    cos, sin = axial_rope_tables(L, DIFF_HEAD_DIM)
    lower_bounds = hgrn_lower_bounds(hgrn_lb)
    silu_c = jax.nn.silu(c)
    silu_cc = jax.nn.silu(c_ctx)
    for i in range(DEPTH_2):
        mixer, slot = i % N_MIXERS, i // N_MIXERS
        ctx_out = i < DEPTH_2 - 1
        ctx_in = ctx_out or mixer != 0
        sh1, sc1, g1, sh2, sc2, g2 = jnp.split((silu_c @ w_mod[i] + b_mod[i])[:, None, :], N_MOD, axis=-1)
        h_lat = modulate(rms_norm(x, norm_g[i, 0]), sh1, sc1)
        h_ctx = None
        if ctx_in:
            csh1, csc1, cg1, csh2, csc2, cg2 = jnp.split(silu_cc @ w_mod[i] + b_mod[i], N_MOD, axis=-1)
            h_ctx = modulate(rms_norm(ctx, norm_g[i, 0]), csh1, csc1)
        if mixer == 0:
            y_lat = fourier_mix(h_lat) @ fnet_w_out[slot]
            y_ctx = fourier_mix(h_ctx) @ fnet_w_out[slot] if ctx_out else None
        elif mixer == 1:
            y_lat, y_ctx = hgrn2_mixer(h_lat, h_ctx, hgrn_w_in[slot], lower_bounds[i], hgrn_gnorm[slot], hgrn_w_out[slot], ctx_out)
        else:
            lambda_init = 0.8 - 0.6 * math.exp(-0.3 * i)
            y_lat, y_ctx = diff_attention(h_lat, h_ctx, diff_w_qkv[slot], diff_lambda[slot], diff_subln[slot], diff_w_out[slot], lambda_init, cos, sin, ctx_out)
        x = x + g1 * rms_norm(y_lat, norm_g[i, 1])
        x = x + g2 * rms_norm(sqrelu_mlp(modulate(rms_norm(x, norm_g[i, 2]), sh2, sc2), w_mlp_in[i], w_mlp_out[i]), norm_g[i, 3])
        if ctx_out:
            ctx = ctx + cg1 * rms_norm(y_ctx, norm_g[i, 1])
            ctx = ctx + cg2 * rms_norm(sqrelu_mlp(modulate(rms_norm(ctx, norm_g[i, 2]), csh2, csc2), w_mlp_in[i], w_mlp_out[i]), norm_g[i, 3])
    return x


def setup_inputs(seed=0):
    out = dict(first_inputs(seed))
    for name, value in second_inputs(seed + 1).items():
        if name != "x":
            out[name + "_2"] = value
    return out


def reference(
    x, mem, positions, pre_norm_g, w_in, q_norm_g, w_uq, kv_norm_g, w_ukv, conv_w, mem_norm_g,
    w_mk, w_mv, w_o, post_norm_g, c_2, ctx_2, c_ctx_2, w_mod_2, b_mod_2, norm_g_2, w_mlp_in_2,
    w_mlp_out_2, fnet_w_out_2, hgrn_w_in_2, hgrn_lb_2, hgrn_gnorm_2, hgrn_w_out_2, diff_w_qkv_2,
    diff_lambda_2, diff_subln_2, diff_w_out_2,
):
    x = first_block(
        x, mem, positions, pre_norm_g, w_in, q_norm_g, w_uq, kv_norm_g, w_ukv, conv_w,
        mem_norm_g, w_mk, w_mv, w_o, post_norm_g,
    )
    return second_block(
        x, c_2, ctx_2, c_ctx_2, w_mod_2, b_mod_2, norm_g_2, w_mlp_in_2, w_mlp_out_2,
        fnet_w_out_2, hgrn_w_in_2, hgrn_lb_2, hgrn_gnorm_2, hgrn_w_out_2, diff_w_qkv_2,
        diff_lambda_2, diff_subln_2, diff_w_out_2,
    )


_drawn_inputs = setup_inputs


def setup_inputs(seed=0):
    import zlib

    import numpy as np

    out = dict(_drawn_inputs(seed))
    spreads = {}
    factors = {'q_norm_g': 8.0, 'kv_norm_g': 8.0, 'mem_norm_g': 8.0, 'b_mod_2': 6.4, 'norm_g_2': 4.31}
    for name, (base, spread) in spreads.items():
        noise = np.random.default_rng([zlib.crc32(name.encode()), seed]).standard_normal(out[name].shape)
        drawn = base * np.exp(spread * noise) if base else spread * noise
        out[name] = __import__('jax').numpy.asarray(drawn.astype(out[name].dtype))
    for name, factor in factors.items():
        out[name] = (out[name] * factor).astype(out[name].dtype)
    return out
```

```python
from contextlib import ExitStack

import concourse.bass as bass
from concourse import mybir

F32 = mybir.dt.float32
F32R = mybir.dt.float32r
I32 = mybir.dt.int32
ALU = mybir.AluOpType
ACT = mybir.ActivationFunctionType
AX_X = mybir.AxisListType.X

P = 128
D = 2048
SEQ = 256
MT = SEQ // P
KT = D // P
DEPTH = 2
HEADS, NOPE, ROPE, VD = 8, 128, 64, 128
QHEAD = NOPE + ROPE
QL, KVL = 512, 256
QLT, KVT = QL // P, KVL // P
CW = 512
CT = CW // P
MH = 4
MIX = HEADS * VD + CW + MH * P
FF = 4 * D
EPS = 1e-6
NMOD = 6
MODCOLS = NMOD * D

C_Q = 0
C_KV = C_Q + QL
C_GB = C_KV + KVL + ROPE
C_GC = C_GB + CW
C_XIN = C_GC + CW
C_QM = C_XIN + CW
C_GATE = C_QM + MH * P

UNITW = 2048
RAW = 4
HIR = 4
CREDIT = 8
AHEAD = 3

GROUPS = (
    [("mk", "FM", 512, 4, 4), ("mv", "TM", 512, 4, 4), ("qlat", "FM", 512, 4, 4), ("kvlat", "FM", 384, 4, 4),
     ("gc", "FM", 512, 4, 4)]
    + [("uq", "UQ", 384, 1, 4)] * 4 + [("ukv", "UKV", 512, 1, 2)] * 4
    + [("xin", "FM", 512, 4, 4), ("gb", "FM", 512, 4, 4), ("qmem", "FM", 512, 4, 4)]
    + [("gate", "FM", 512, 4, 4)] * 4 + [("wo", "TM", 512, 4, 4)] * 4
)
NG = len(GROUPS)
UNIT_AT = [sum(g[3] for g in GROUPS[:i]) for i in range(NG + 1)]
LU = UNIT_AT[-1]
LH = 2 * LU
H_AT = [2 * u for u in UNIT_AT]
G_OF = {name: i for i, name in reversed(list(enumerate(g[0] for g in GROUPS)))}
assert LU % RAW == 0 and LH % HIR == 0 and NG % 2 == 0


def group_of(s):
    return max(g for g in range(NG) if H_AT[g] <= s)


ACT_READS = [g for g in range(NG) if GROUPS[g][0] not in ("xin", "gb")]
DVE_READS = [g for g in range(NG) if GROUPS[g][0] in ("uq", "xin", "gb", "gate")]
READS_ACT, READS_DVE = len(ACT_READS), len(DVE_READS)

MU = 96
MCH = MU // 8
MRING = 3


def mod_unit(s):
    return MOD_AT.index(s) if s in MOD_AT else None


GATE_PART = (2, 0, 1, 3)

QK_AT = [59 + 3 * h for h in range(HEADS)] + [84 + 3 * h for h in range(MH)]
NH = HEADS + MH
PT_LAG, PV_LAG = 4, 6
SUM_LAG, ROT_LAG, ROW_LAG, HI_LAG = 2, 4, 7, 8
C_CONV = 2 * KT + QLT + KVT
G_CONST = C_CONV + 3 * CT + 10

MOD_AT = [s for s in range(LH) if not H_AT[G_OF["uq"]] <= s < H_AT[G_OF["xin"]] + 2 and s % 8][:MU]
LAT_AT = (H_AT[G_OF["gc"] - 1], H_AT[G_OF["gc"]] + 1)
M3_BUSY = [q + PV_LAG for q in QK_AT] + [LAT_AT[1] + ROW_LAG] + list(range(6, 14))
MOD_T_AT = [min(t for t in range(MOD_AT[8 * c + 7] + 4, LH + 1) if t - 1 not in M3_BUSY) for c in range(MCH)]
ENDED = {H_AT[g + 1]: g for g in range(NG)}
PI = 3.1415925
INV_TURN = 0.15915494309189535
ROUNDER = 12582912.0
TURN_PARTS = (6.28125, 0.001934051513671875, 1.255422830581665e-06, 2.430840251310684e-10)


def half_of(s):
    g = GROUPS[group_of(s)]
    return g[2] * g[4] // 2


def build_program(nc, x, mem, positions, small, w_in, w_uq, w_ukv, w_mk, w_mv, w_o, post_g,
                  consts, rope_c, dft, cvec, bmod, ng2, w_mod, w_fnet, w_mlp_in, w_mlp_out, out):
    scratch = nc.dram_tensor("mod_rows", [64, P], F32).ap()
    ctx = ExitStack()
    with ctx:
        origin = nc.sbuf_base + (-nc.sbuf_base) % 64

        def at(name, shape, kb, dt=F32):
            return nc.alloc_sbuf_tensor_at(name, shape, dt, offset=origin + int(kb * 1024))

        def sem(name):
            return ctx.enter_context(nc.semaphore(name))

        Hhi = at("Hhi", [P, KT, SEQ], 0, F32R)
        Hlo = at("Hlo", [P, KT, SEQ], 16, F32R)
        Yhi = at("Yhi", [P, KT, SEQ], 32, F32R)
        Ylo = at("Ylo", [P, KT, SEQ], 48, F32R)
        raw = [at(f"raw{i}", [P, UNITW], 64 + 8 * i) for i in range(RAW)]
        wlo = [at(f"wlo{i}", [P, UNITW], 64 + 8 * i, F32R) for i in range(RAW)]
        whi = [at(f"whi{i}", [P, UNITW // 2], 96 + 4 * i, F32R) for i in range(HIR)]
        X = at("X", [P, MT, D], 112)
        A = 128
        qlh = at("qlh", [P, QLT, SEQ], A, F32R)
        qll = at("qll", [P, QLT, SEQ], A + 4, F32R)
        kvh = at("kvh", [P, KVT, SEQ], A + 8, F32R)
        kvl = at("kvl", [P, KVT, SEQ], A + 10, F32R)
        prob = at("prob", [P, 2, MT, SEQ], A)
        probT = at("probT", [P, MT, SEQ], A + 4)
        U = at("U", [P, CT, SEQ + 2], A + 6)
        junk = at("junk", [P, D], A)
        rows = at("rows", [64, P], A)
        O = at("O", [P, KT, SEQ], A + 12)
        qpe = at("qpe", [P, HEADS // 2, SEQ], A + 28)
        kn = at("kn", [P, HEADS, SEQ], A + 32)
        kpe = at("kpe", [P, SEQ], A + 40)
        V = at("V", [P, MT, HEADS * VD], A + 41)
        mkT = at("mkT", [P, MH, SEQ], A + 49)
        mv = at("mv", [P, MT, MH * P], A + 53)
        cosT = at("cosT", [P, SEQ], A + 57)
        sinT = at("sinT", [P, SEQ], A + 58)
        swap = at("swap", [P, SEQ], A + 59)
        rtmp = at("rtmp", [P, SEQ], A + 60)
        pos = at("pos", [P, SEQ], A + 59, I32)
        rot = at("rot", [P, MT, P], A + 59)
        rawlat = at("rawlat", [P, QLT + KVT, SEQ], A + 32)
        sqlat = at("sqlat", [P, QLT + KVT, SEQ], A + 41)
        xn = at("xn", [P, MT, D], A + 12)
        otok = at("otok", [P, MT, D], A + 12)
        memx = at("memx", [P, MT, D], A + 28)
        post = at("post", [P, D], A + 44)
        gate = at("gate", [P, CT, SEQ], A + 6)
        AB = at("AB", [P, KT, 2 * SEQ], 32)
        rowb = [at(f"rowb{i}", [P, D], A + 28 + 8 * i) for i in range(4)]
        rel = at("rel", [P, CT, SEQ], A + 28)
        sqr = at("sqr", [P, CT, SEQ], A + 32)
        vtmp = at("vtmp", [P, 4, SEQ], A + 36)
        modw = [at(f"modw{i}", [P, 1024], A + 61 + 4 * i) for i in range(MRING)]
        cs = at("cs", [P, MT, 2 * SEQ], A + 61)
        modacc = at("modacc", [P, 2, 512], A + 73)
        m = A + 77
        ident = at("ident", [P, P], m)
        ones = at("ones", [P, 8], m + 0.5)
        gs = at("gs", [P, G_CONST], m + 0.5625)
        modT = at("modT", [P, NMOD * KT], m + 0.8125)
        ngs = at("ngs", [P, 4 * KT], m + 1.1875)
        R = at("R", [P, 4 * KT], m + 1.4375)
        A2 = at("A2", [P, KT], m + 1.6875)
        cv = at("cv", [P, 3 * KT], m + 1.75)
        ropev = at("ropev", [P, 2], m + 1.9375)
        sc = at("sc", [P, 64], m + 1.96875)
        SS, MS, RS = 0, 4, 8
        LS, LM, LR = 12, 16, 20
        NM, RSUM, RINV = 24, 28, 32
        PS = 36
        OS, OM, OR = 44, 46, 48
        POW, EPSC, MX = 50, 52, 54
        assert origin + (m + 2.25) * 1024 <= nc.sbuf_top

        acc = [ctx.enter_context(nc.psum_tensor(f"acc{i}", [P, 1024], F32)) for i in range(2)]
        M = [ctx.enter_context(nc.psum_tensor(f"M{i}", [P, 512], F32)) for i in range(4)]
        MODCOL = 480

        raw_in = [sem(f"raw_in{i}") for i in range(RAW)]
        hi_ready, lo_ready = sem("hi_ready"), sem("lo_ready")
        half_used = sem("half_used")
        acc_act, acc_dve = sem("acc_act"), sem("acc_dve")
        ident_in, x_in, small_in, mem_in, post_in = map(sem, ("ident_in", "x_in", "small_in", "mem_in", "post_in"))
        vec_in, rope_in, c_in, dft_in = map(sem, ("vec_in", "rope_in", "c_in", "dft_in"))
        ones_set, pow_set = sem("ones_set"), sem("pow_set")
        rope_step, ang_ready, sin_ready, c_exp, c_ready = map(sem, ("rope_step", "ang_ready", "sin_ready", "c_exp", "c_ready"))
        tables_ready = sem("tables_ready")
        sq_step, pool_step = sem("sq_step"), sem("pool_step")
        mem_ss, mem_rstd, mem_xn, mem_T, mem_hi, mem_lo = map(sem, ("mem_ss", "mem_rstd", "mem_xn", "mem_T", "mem_hi", "mem_lo"))
        x_ss, x_rstd, x_xn, x_T, x_hi, x_lo = map(sem, ("x_ss", "x_rstd", "x_xn", "x_T", "x_hi", "x_lo"))
        layer_done = sem("layer_done")
        LN = ("raw", "sq", "sum", "ss", "rstd", "rot", "row", "val", "hi", "lo")
        lat = [{n: sem(f"{w}_{n}") for n in LN} for w in ("q", "kv")]
        swap_in, rope_prod, rope_out, kv_out = map(sem, ("swap_in", "rope_prod", "rope_out", "kv_out"))
        gc_out, u_ready, conv_step, qm_out = map(sem, ("gc_out", "u_ready", "conv_step", "qm_out"))
        S_ready, mx_ready, nm_ready, exp_ready, inv_ready, P_ready, PT_done, PT_out, PV_done, o_out = map(sem, (
            "S_ready", "mx_ready", "nm_ready", "exp_ready", "inv_ready", "P_ready", "PT_done", "PT_out", "PV_done", "o_out"))
        g_tanh, g_step, y_val, y_hi, y_lo = map(sem, ("g_tanh", "g_step", "y_val", "y_hi", "y_lo"))
        wo_sq, wo_out, o_ss, o_rstd, upd_step = map(sem, ("wo_sq", "wo_out", "o_ss", "o_rstd", "upd_step"))
        mod_in = [sem(f"mod_in{i}") for i in range(MRING)]
        mod_used, mod_step, mod_T, mod_out = map(sem, ("mod_used", "mod_step", "mod_T", "mod_out"))
        r_ready, r_T, rows_ready, rows_out = map(sem, ("r_ready", "r_T", "rows_ready", "rows_out"))
        row_in = [sem(f"row_in{i}") for i in range(4)]
        h_step, h_ready, ab_ps, ab_act, ab_dve, f_ps, f_hi, f_lo = map(sem, (
            "h_step", "h_ready", "ab_ps", "ab_act", "ab_dve", "f_ps", "f_hi", "f_lo"))
        x2_T, x2_val, x2_hi, x2_lo = map(sem, ("x2_T", "x2_val", "x2_hi", "x2_lo"))
        m_rel, m_sq, m_hi, m_lo, y_zero = map(sem, ("m_rel", "m_sq", "m_hi", "m_lo", "y_zero"))
        stored = sem("stored")

        FN_H, ML_H = DEPTH * LH, DEPTH * LH + 32
        ACT0, DVE0 = DEPTH * READS_ACT, DEPTH * READS_DVE

        def load_unit(sp, base, u, dst, src):
            sp.wait_ge(half_used, base + 2 * (u - RAW) + 2 + CREDIT)
            sp.dma_start(dst, src).then_inc(raw_in[u % RAW], 16)

        def weight_rows(w, k0, nk, c0, n):
            return w[k0 * P:(k0 + nk) * P, c0:c0 + n].rearrange("(k p) n -> p k n", p=P)

        def slot(u, nk, n):
            return raw[u % RAW][:, 0:nk * n].rearrange("p (k n) -> p k n", k=nk)

        def split_hi(act, base, s, n):
            u = s // 2
            act.wait_ge(raw_in[u % RAW], 2 * base + 16 * (u // RAW + 1))
            act.wait_ge(half_used, base + s - HIR + 1 + CREDIT)
            nc.scalar.activation(whi[s % HIR][:, 0:n], raw[u % RAW][:, (s % 2) * n:(s % 2) * n + n],
                                 ACT.Copy).then_inc(hi_ready, 1)

        def split_lo(dve, base, s, n):
            u = s // 2
            dve.wait_ge(hi_ready, base + s + 1)
            part = slice((s % 2) * n, (s % 2) * n + n)
            nc.vector.tensor_tensor(wlo[u % RAW][:, part], raw[u % RAW][:, part],
                                    whi[s % HIR][:, 0:n].bitcast(F32), ALU.subtract).then_inc(lo_ready, 1)

        def mm(o, a, b, start, stop):
            return nc.tensor.matmul(o, a, b, start=start, stop=stop, skip_group_check=True)

        def halves(s, width, nk):
            n = nk * width
            hi = whi[s % HIR][:, 0:n].rearrange("p (k n) -> p k n", n=width)
            lo = wlo[s // 2 % RAW][:, (s % 2) * n:(s % 2) * n + n].rearrange("p (k n) -> p k n", n=width)
            return hi, lo

        def fm_half(s, ps, act_in, cols, k0, nk, first, last, width):
            hi, lo = halves(s, width, nk)
            ah, al = act_in
            for kk in range(nk):
                k = k0 + kk
                for t, col in enumerate(cols):
                    o = ps[:, t * SEQ:(t + 1) * SEQ]
                    mm(o, col(hi[:, kk, :]), ah[:, k, :], first and kk == 0 and t % 2 == 0, False)
                    mm(o, col(hi[:, kk, :]), al[:, k, :], False, False)
                    w = mm(o, col(lo[:, kk, :]), ah[:, k, :], False, last and kk == nk - 1)
            return w

        def tm_half(s, ps, act_in, k0, nk, first, last, width):
            hi, lo = halves(s, width, nk)
            ah, al = act_in
            for kk in range(nk):
                k = k0 + kk
                for t in range(MT):
                    o = ps[:, t * width:(t + 1) * width]
                    tok = slice(t * P, (t + 1) * P)
                    mm(o, ah[:, k, tok], hi[:, kk, :], first and kk == 0, False)
                    mm(o, ah[:, k, tok], lo[:, kk, :], False, False)
                    w = mm(o, al[:, k, tok], hi[:, kk, :], False, last and kk == nk - 1)
            return w

        def ukv_half(s, ps, k, first, last):
            hi, lo = halves(s, 512, 1)
            fm_half(s, ps, (kvh, kvl), [lambda w: w[:, 0:NOPE], lambda w: w[:, 256:256 + NOPE]], k, 1, first, last, 512)

            def vcols(w):
                return w[:, 0, :].rearrange("p (h c) -> p h c", h=2)[:, :, NOPE:NOPE + VD]

            for t in range(MT):
                o = ps[:, 512 + t * SEQ:512 + (t + 1) * SEQ].rearrange("p (h c) -> p h c", h=2)
                tok = slice(t * P, (t + 1) * P)
                mm(o, kvh[:, k, tok], vcols(hi), first and t == 0, False)
                mm(o, kvh[:, k, tok], vcols(lo), False, False)
                w = mm(o, kvl[:, k, tok], vcols(hi), False, last)
            return w

        four = [lambda w, t=t: w[:, t * P:(t + 1) * P] for t in range(4)]

        def norm_T(src, f):
            for t in range(MT):
                w = nc.tensor.transpose(M[f % 4][:, t * P:(t + 1) * P], src[:, t, f * P:(f + 1) * P], ident[:, :])
            return w

        block = ctx.enter_context(nc.Block())

        @block.sync
        def _(sp):
            sp.dma_start(ident[:, :], consts).then_inc(ident_in, 16)
            sp.dma_start(X[:, :, :], x.rearrange("(t p) d -> p t d", p=P)).then_inc(x_in, 16)
            with sp.Fori(0, DEPTH) as l:
                sp.wait_ge(layer_done, l + 1)
                sp.dma_start(memx[:, :, :], mem.rearrange("(t p) d -> p t d", p=P)).then_inc(mem_in, 16)
                sp.dma_start(gs[:, :], small[bass.ds(l, 1), :, :].rearrange("a p n -> p (a n)")).then_inc(small_in, 16)

                def of_layer(w):
                    return w[bass.ds(l, 1)].rearrange("a k n -> (a k) n")

                w_in_l = of_layer(w_in)
                src = {"mk": (of_layer(w_mk), 0), "mv": (of_layer(w_mv), 0), "qlat": (w_in_l, C_Q), "kvlat": (w_in_l, C_KV),
                       "gc": (w_in_l, C_GC), "uq": (of_layer(w_uq), 0), "ukv": (of_layer(w_ukv), 0), "xin": (w_in_l, C_XIN),
                       "gb": (w_in_l, C_GB), "qmem": (w_in_l, C_QM), "gate": (w_in_l, C_GATE), "wo": (of_layer(w_o), 0)}
                for g, (name, kind, width, units, nk) in enumerate(GROUPS):
                    w, c0 = src[name]
                    for i in range(units):
                        u = UNIT_AT[g] + i
                        if name == "gate":
                            c0 = C_GATE + (GATE_PART[g - G_OF[name]] - (g - G_OF[name])) * width
                        load_unit(sp, l * LH, u, slot(u, nk, width),
                                  weight_rows(w, i * nk, nk, c0 + (g - G_OF[name]) * width, width))
                    if g == G_OF["wo"] - 1:
                        sp.wait_ge(o_out, l * NH + NH)
                        sp.dma_start(post[:, :], post_g[bass.ds(l, 1), :].partition_broadcast(P)).then_inc(post_in, 16)
            for i in range(4):
                load_unit(sp, FN_H, i, slot(i, 4, 512), weight_rows(w_fnet, 4 * i, 4, 0, 512))
            sp.wait_ge(mod_used, DEPTH * MU + MRING)
            sp.dma_start(cs[:, :, :], dft.rearrange("(t p) n -> p t n", p=P)).then_inc(dft_in, 16)
            sp.wait_ge(rows_ready, 1)
            sp.dma_start(scratch, rows[:, :]).then_inc(rows_out, 16)
            sp.wait_ge(rows_out, 16)
            sp.wait_ge(layer_done, DEPTH + 1)
            for i in range(4):
                row = scratch[i * KT:(i + 1) * KT, :].rearrange("k p -> (k p)")
                sp.dma_start(rowb[i][:, :], row.partition_broadcast(P)).then_inc(row_in[i], 16)
            for n in range(1, 4):
                for i in range(4):
                    u = 4 * n + i
                    load_unit(sp, FN_H, u, slot(u, 4, 512), weight_rows(w_fnet, 4 * i, 4, 512 * n, 512))
            with sp.Fori(0, 4) as q:
                w1 = w_mlp_in.rearrange("k (q n) -> q k n", q=4)[bass.ds(q, 1)].rearrange("a k n -> (a k) n")
                w2 = w_mlp_out.rearrange("(q k) n -> q k n", q=4)[bass.ds(q, 1)].rearrange("a k n -> (a k) n")
                for n in range(8):
                    for i in range(4):
                        u = 4 * n + i
                        load_unit(sp, ML_H + 64 * q, u, slot(u, 4, 512),
                                  weight_rows(w1 if n < 4 else w2, 4 * i, 4, 512 * (n % 4), 512))
            sp.wait_ge(layer_done, DEPTH + 3)
            sp.dma_start(out.rearrange("(t p) d -> p t d", p=P), X[:, :, :]).then_inc(stored, 16)
            sp.wait_ge(stored, 16)

        @block.gpsimd
        def _(pool):
            nc.gpsimd.memset(ones[:, :], 1.0).then_inc(ones_set, 1)
            nc.gpsimd.memset(sc[:, POW:POW + 2], -0.5).then_inc(pow_set, 1)
            nc.gpsimd.memset(sc[:, EPSC:EPSC + 2], EPS).then_inc(pow_set, 1)
            pool.wait_ge(pow_set, 2)

            def rstd(s0, m0, r0, step, done):
                nc.gpsimd.tensor_tensor(sc[:, m0:m0 + 2], sc[:, s0:s0 + 2], sc[:, EPSC:EPSC + 2], ALU.add).then_inc(pool_step, 1)
                pool.wait_ge(pool_step, step)
                nc.gpsimd.tensor_tensor(sc[:, r0:r0 + 2], sc[:, m0:m0 + 2], sc[:, POW:POW + 2], ALU.pow).then_inc(done, 1)

            with pool.Fori(0, DEPTH) as l:
                w = w_mod.rearrange("k (l n) -> l k n", l=DEPTH)[bass.ds(l, 1)].rearrange("a k n -> (a k) n")

                def load_mod(j):
                    pool.wait_ge(mod_used, l * MU + j + 1)
                    pool.dma_start(modw[j % MRING][:, :].rearrange("p (k n) -> p k n", k=2),
                                   weight_rows(w, 2 * (j % 8), 2, 512 * (j // 8), 512)).then_inc(mod_in[j % MRING], 16)

                pool.wait_ge(mem_ss, l + 1)
                rstd(SS, MS, RS, l * 5 + 1, mem_rstd)
                pool.wait_ge(x_ss, l + 1)
                rstd(SS + 2, MS + 2, RS + 2, l * 5 + 2, x_rstd)
                for s in range(LH):
                    if s == LAT_AT[0] + SUM_LAG + 3:
                        pool.wait_ge(lat[0]["ss"], l + 1)
                        rstd(LS, LM, LR, l * 5 + 3, lat[0]["rstd"])
                    if s == LAT_AT[1] + SUM_LAG + 3:
                        pool.wait_ge(lat[1]["ss"], l + 1)
                        rstd(LS + 2, LM + 2, LR + 2, l * 5 + 4, lat[1]["rstd"])
                    if mod_unit(s) is not None:
                        load_mod(mod_unit(s))
                pool.wait_ge(o_ss, l + 1)
                rstd(OS, OM, OR, l * 5 + 5, o_rstd)
            pool.wait_ge(x_ss, DEPTH + 1)
            rstd(SS + 2, MS + 2, RS + 2, DEPTH * 5 + 1, x_rstd)
            pool.wait_ge(o_ss, DEPTH + 1)
            rstd(OS, OM, OR, DEPTH * 5 + 2, o_rstd)
            pool.wait_ge(x_ss, DEPTH + 2)
            rstd(SS + 2, MS + 2, RS + 2, DEPTH * 5 + 3, x_rstd)
            pool.wait_ge(o_ss, DEPTH + 2)
            rstd(OS, OM, OR, DEPTH * 5 + 4, o_rstd)

        @block.scalar
        def _(act):
            def squares(src, c, at_step, done):
                for t in range(MT):
                    act.wait_ge(sq_step, at_step + t + 1)
                    w = nc.scalar.activation(junk[:, :], src[:, t, :], ACT.Square, scale=D ** -0.5, accum_out=sc[:, c + t:c + t + 1])
                    w.then_inc(sq_step, 1)
                act.wait_ge(sq_step, at_step + MT + 1)
                act.sem_inc(done, 1)

            def flat(ap):
                return ap.rearrange("p h n -> p (h n)")

            def rows_out_of(a, n):
                for t in range(MT):
                    part = a[:, t * 512:(t + 1) * 512]
                    nc.scalar.activation(otok[:, t, n * 512:(n + 1) * 512], part, ACT.Copy)
                    w = nc.scalar.activation(junk[:, t * 512 + 1024 * (n % 2):(t + 1) * 512 + 1024 * (n % 2)], part, ACT.Square, scale=D ** -0.5,
                                             accum_out=sc[:, PS + 4 * t + n:PS + 4 * t + n + 1])
                return w

            act.dma_start(modT[:, :], bmod).then_inc(vec_in, 16)
            act.dma_start(ngs[:, :], ng2).then_inc(vec_in, 16)
            act.dma_start(ropev[:, :], rope_c).then_inc(rope_in, 16)
            act.dma_start(pos[:, :], positions.partition_broadcast(P)).then_inc(rope_in, 16)
            act.dma_start(cv[:, 0:KT], cvec).then_inc(c_in, 16)
            act.wait_ge(ang_ready, 1)
            nc.scalar.activation(swap[:, :], sinT[:, :], ACT.Sin).then_inc(sin_ready, 1)
            nc.scalar.activation(rtmp[:, :], cosT[:, :], ACT.Sin).then_inc(sin_ready, 1)
            act.wait_ge(c_in, 16)
            nc.scalar.activation(cv[:, KT:2 * KT], cv[:, 0:KT], ACT.Exp, scale=-1.0).then_inc(c_exp, 1)
            act.sem_inc(sq_step, 1)
            act.wait_ge(x_in, 16)

            with act.Fori(0, DEPTH) as l:
                base = l * LH
                act.wait_ge(mem_in, 16 * l + 16)
                squares(memx, SS, l * 4, mem_ss)
                act.wait_ge(layer_done, l + 1)
                squares(X, SS + 2, l * 4 + 2, x_ss)
                act.wait_ge(small_in, 16 * l + 16)
                for f in range(KT):
                    act.wait_ge(mem_T, l * KT + f + 1)
                    nc.scalar.activation(Yhi[:, f, :], M[f % 4][:, 0:SEQ], ACT.Copy,
                                         scale=gs[:, KT + f:KT + f + 1]).then_inc(mem_hi, 1)
                for s in range(AHEAD):
                    split_hi(act, base, s, 1024)
                for s in range(LH + 1):
                    if s + AHEAD < LH:
                        split_hi(act, base, s + AHEAD, half_of(s + AHEAD))
                    if 6 <= s < 14:
                        for f in (2 * (s - 6), 2 * (s - 6) + 1):
                            act.wait_ge(x_T, l * KT + f + 1)
                            nc.scalar.activation(Hhi[:, f, :], M[f % 4][:, 0:SEQ], ACT.Copy,
                                                 scale=gs[:, f:f + 1]).then_inc(x_hi, 1)
                    for w, nt in ((0, QLT), (1, KVT)):
                        if s == LAT_AT[w] + HI_LAG:
                            act.wait_ge(lat[w]["val"], l + 1)
                            o, i = (qlh, 0) if w == 0 else (kvh, QLT)
                            nc.scalar.activation(flat(o[:, :, :]), flat(rawlat[:, i:i + nt, :]), ACT.Copy).then_inc(lat[w]["hi"], 1)
                    g = ENDED.get(s)
                    name = GROUPS[g][0] if g is not None else None
                    if name is not None:
                        a = acc[g % 2]
                        i = g - G_OF[name]
                        act.wait_ge(half_used, base + s + CREDIT)
                    if name == "mk":
                        nc.scalar.activation(flat(mkT[:, :, :]), a[:, :], ACT.Copy).then_inc(acc_act, 1)
                    if name == "mv":
                        nc.scalar.activation(flat(mv[:, :, :]), a[:, :], ACT.Copy).then_inc(acc_act, 1)
                    if name == "qlat":
                        act.wait_ge(x_xn, l + 1)
                        nc.scalar.activation(flat(rawlat[:, 0:QLT, :]), a[:, :], ACT.Copy).then_inc(lat[0]["raw"], 1)
                        act.wait_ge(lat[0]["raw"], l + 1)
                        act.sem_inc(acc_act, 1)
                    if name == "kvlat":
                        nc.scalar.activation(flat(rawlat[:, QLT:, :]), a[:, 0:512], ACT.Copy).then_inc(lat[1]["raw"], 1)
                        for b in range(4):
                            h = 32 * (b % 2)
                            nc.scalar.activation(rtmp[32 * b:32 * b + 32, :], a[h:h + 32, 512:768], ACT.Copy)
                            w = nc.scalar.activation(swap[32 * b:32 * b + 32, :], a[32 - h:64 - h, 512:768], ACT.Copy)
                        w.then_inc(swap_in, 1)
                        act.wait_ge(swap_in, 5 * l + 1)
                        act.sem_inc(acc_act, 1)
                    if name == "gc":
                        nc.scalar.activation(flat(O[:, HEADS:HEADS + CT, :]), a[:, :], ACT.Copy).then_inc(acc_act, 1)
                    if name == "uq":
                        act.wait_ge(rope_out, l * 5 + i + 1)
                        for b in range(4):
                            w = nc.scalar.activation(swap[32 * b:32 * b + 32, :], a[32 * (b ^ 1):32 * (b ^ 1) + 32, 512:768], ACT.Copy)
                        w.then_inc(swap_in, 1)
                        nc.scalar.activation(flat(O[:, 2 * i:2 * i + 2, :]), a[:, 0:512], ACT.Copy).then_inc(acc_act, 1)
                    if name == "ukv":
                        nc.scalar.activation(V[:, :, 256 * i:256 * i + 256],
                                             a[:, 512:1024].rearrange("p (t n) -> p t n", t=MT), ACT.Copy)
                        nc.scalar.activation(flat(kn[:, 2 * i:2 * i + 2, :]), a[:, 0:512], ACT.Copy).then_inc(acc_act, 1)
                    if name == "qmem":
                        nc.scalar.activation(flat(O[:, HEADS + CT:, :]), a[:, :], ACT.Copy).then_inc(acc_act, 1)
                    if name == "gate":
                        if i:
                            act.wait_ge(y_lo, l * 4 + i)
                        nc.scalar.activation(flat(gate[:, :, :]), a[:, :], ACT.Tanh, scale=0.5).then_inc(g_tanh, 1)
                        act.wait_ge(g_tanh, l * 4 + i + 1)
                        act.sem_inc(acc_act, 1)
                    if name == "wo":
                        rows_out_of(a, i).then_inc(acc_act, 1)
                    for i in range(4):
                        if s == H_AT[G_OF["gate"] + i + 1] + 2:
                            act.wait_ge(y_val, l * 4 + i + 1)
                            part = GATE_PART[i]
                            nc.scalar.activation(Yhi[:, 4 * part:4 * part + 4, :], gate[:, :, :], ACT.Copy).then_inc(y_hi, 1)
                    for h in range(NH):
                        b = h % 2
                        if s == QK_AT[h]:
                            act.wait_ge(nm_ready, l * NH + h + 1)
                            scale = float(QHEAD if h < HEADS else P) ** -0.5
                            for t in range(MT):
                                w = nc.scalar.activation(prob[:, b, t, :], M[b][:, t * SEQ:(t + 1) * SEQ], ACT.Exp, scale=scale,
                                                         bias=sc[:, NM + 2 * b + t:NM + 2 * b + t + 1],
                                                         accum_out=sc[:, RSUM + 2 * b + t:RSUM + 2 * b + t + 1])
                            w.then_inc(exp_ready, 1)
                        if s == QK_AT[h] + PT_LAG:
                            act.wait_ge(PT_done, l * NH + h + 1)
                            nc.scalar.activation(flat(probT[:, :, :]), M[2][:, :], ACT.Copy).then_inc(PT_out, 1)
            act.wait_ge(r_T, 1)
            nc.scalar.activation(rows[:, :], M[0][0:64, 0:P], ACT.Copy).then_inc(rows_ready, 1)
            act.wait_ge(rows_out, 16)
            act.wait_ge(layer_done, DEPTH + 1)
            squares(X, SS + 2, DEPTH * 4, x_ss)
            for f in range(KT):
                act.wait_ge(ab_ps, f + 1)
                nc.scalar.activation(AB[:, f, 0:SEQ], M[f % 4][:, 0:SEQ], ACT.Copy).then_inc(ab_act, 1)
            for s in range(AHEAD):
                split_hi(act, FN_H, s, 1024)
            for f in range(KT):
                act.wait_ge(f_ps, f + 1)
                nc.scalar.activation(Hhi[:, f, :], M[f % 4][:, 0:SEQ], ACT.Copy).then_inc(f_hi, 1)
            for s in range(33):
                if s + AHEAD < 32:
                    split_hi(act, FN_H, s + AHEAD, 1024)
                if s and s % 8 == 0:
                    act.wait_ge(half_used, FN_H + s + CREDIT)
                    rows_out_of(acc[(s // 8 - 1) % 2], s // 8 - 1).then_inc(acc_act, 1)
            act.wait_ge(layer_done, DEPTH + 2)
            squares(X, SS + 2, DEPTH * 4 + 2, x_ss)
            for f in range(KT):
                act.wait_ge(x2_val, f + 1)
                nc.scalar.activation(Hhi[:, f, :], vtmp[:, f % 4, :], ACT.Copy).then_inc(x2_hi, 1)
            with act.Fori(0, 4) as q:
                base = ML_H + 64 * q
                for s in range(AHEAD):
                    split_hi(act, base, s, 1024)
                for s in range(64):
                    if s + AHEAD < 64:
                        split_hi(act, base, s + AHEAD, 1024)
                    if s in (8, 16, 24, 32):
                        j = s // 8 - 1
                        act.wait_ge(half_used, base + s + CREDIT)
                        nc.scalar.activation(flat(rel[:, :, :]), acc[j % 2][:, :], ACT.Relu).then_inc(m_rel, 1)
                        act.wait_ge(m_sq, 4 * q + j + 1)
                        nc.scalar.activation(Yhi[:, 4 * j:4 * j + 4, :], sqr[:, :, :], ACT.Copy).then_inc(m_hi, 1)
            act.wait_ge(acc_dve, DVE0 + 16 + 1)
            squares(otok, OS, DEPTH * 4 + 4, o_ss)

        @block.vector
        def _(dve):
            def flat(ap):
                return ap.rearrange("p h n -> p (h n)")

            def tt(o, a, b, op):
                return nc.vector.tensor_tensor(o, a, b, op)

            def step(ins, n):
                ins.then_inc(rope_step, 1)
                dve.wait_ge(rope_step, n)

            dve.wait_ge(rope_in, 32)
            step(nc.vector.tensor_copy(rtmp[:, :], pos[:, :]), 1)
            step(nc.vector.tensor_scalar(sinT[:, :], rtmp[:, :], ropev[:, 0:1], None, ALU.mult), 2)
            step(nc.vector.tensor_scalar(cosT[:, :], sinT[:, :], INV_TURN, ROUNDER, ALU.mult, ALU.add), 3)
            step(nc.vector.tensor_scalar(cosT[:, :], cosT[:, :], ROUNDER, None, ALU.subtract), 4)
            for i, part in enumerate(TURN_PARTS):
                step(nc.vector.scalar_tensor_tensor(sinT[:, :], cosT[:, :], -part, sinT[:, :], ALU.mult, ALU.add), 5 + i)
            n = 5 + len(TURN_PARTS)
            step(nc.vector.tensor_scalar(sinT[:, :], sinT[:, :], -PI, PI, ALU.max, ALU.min), n)
            nc.vector.tensor_scalar(cosT[:, :], sinT[:, :], 0.5, None, ALU.mult).then_inc(ang_ready, 1)
            dve.wait_ge(sin_ready, 2)
            nc.vector.tensor_scalar(sinT[:, :], swap[:, :], ropev[:, 1:2], None, ALU.mult)
            step(tt(cosT[:, :], rtmp[:, :], rtmp[:, :], ALU.mult), n + 1)
            step(nc.vector.tensor_scalar(cosT[:, :], cosT[:, :], -2.0, 1.0, ALU.mult, ALU.add), n + 2)
            dve.wait_ge(c_exp, 1)
            step(nc.vector.tensor_scalar(cv[:, KT:2 * KT], cv[:, KT:2 * KT], 1.0, None, ALU.add), n + 3)
            step(nc.vector.reciprocal(cv[:, 2 * KT:], cv[:, KT:2 * KT]), n + 4)
            step(tt(cv[:, 2 * KT:], cv[:, 2 * KT:], cv[:, 0:KT], ALU.mult), n + 5)
            dve.wait_ge(vec_in, 32)
            dve.wait_ge(x_in, 16)
            dve.sem_inc(layer_done, 1)
            dve.sem_inc(mod_used, MRING)

            def residual(gain, n, done_at):
                for t in range(MT):
                    nc.vector.scalar_tensor_tensor(otok[:, t, :], otok[:, t, :], sc[:, OR + t:OR + t + 1], gain[:, :],
                                                   ALU.mult, ALU.mult).then_inc(upd_step, 1)
                for t in range(MT):
                    dve.wait_ge(upd_step, done_at + t + 1)
                    w = tt(X[:, t, :], X[:, t, :], otok[:, t, :], ALU.add)
                w.then_inc(layer_done, 1)
                dve.wait_ge(layer_done, n + 2)

            def row_sums():
                return nc.vector.tensor_reduce(sc[:, OS:OS + 2], sc[:, PS:PS + 8].rearrange("p (t n) -> p t n", t=MT), AX_X, ALU.add)

            with dve.Fori(0, DEPTH) as l:
                base = l * LH
                dve.wait_ge(mem_rstd, l + 1)
                for t in range(MT):
                    w = nc.vector.tensor_scalar(memx[:, t, :], memx[:, t, :], sc[:, RS + t:RS + t + 1], None, ALU.mult)
                w.then_inc(mem_xn, 1)
                dve.wait_ge(x_rstd, l + 1)
                for t in range(MT):
                    w = nc.vector.tensor_scalar(xn[:, t, :], X[:, t, :], sc[:, RS + 2 + t:RS + 3 + t], None, ALU.mult)
                w.then_inc(x_xn, 1)
                for f in range(KT):
                    dve.wait_ge(mem_hi, l * KT + f + 1)
                    nc.vector.scalar_tensor_tensor(Ylo[:, f, :], M[f % 4][:, 0:SEQ], gs[:, KT + f:KT + f + 1],
                                                   Yhi[:, f, :].bitcast(F32), ALU.mult, ALU.subtract).then_inc(mem_lo, 1)
                for s in range(AHEAD):
                    split_lo(dve, base, s, 1024)
                for s in range(LH + 1):
                    if s + AHEAD < LH:
                        split_lo(dve, base, s + AHEAD, half_of(s + AHEAD))
                    if s in MOD_T_AT:
                        c = MOD_T_AT.index(s)
                        dve.wait_ge(mod_T, l * MCH + c + 1)
                        cols = modT[:, bass.ds(l * 4 * MCH + 4 * c, 4)]
                        tt(cols, M[3][:, MODCOL:MODCOL + 4], cols, ALU.add).then_inc(mod_out, 1)
                    if 6 <= s < 14:
                        for f in (2 * (s - 6), 2 * (s - 6) + 1):
                            dve.wait_ge(x_hi, l * KT + f + 1)
                            nc.vector.scalar_tensor_tensor(Hlo[:, f, :], M[f % 4][:, 0:SEQ], gs[:, f:f + 1],
                                                           Hhi[:, f, :].bitcast(F32), ALU.mult, ALU.subtract).then_inc(x_lo, 1)
                    j = mod_unit(s)
                    if j is not None:
                        c = j // 8
                        dve.wait_ge(mod_in[j % MRING], MU // MRING * 16 * l + 16 * (j // MRING + 1))
                        if j % 8 == 0 and c >= 2:
                            dve.wait_ge(mod_T, l * MCH + c - 1)
                        for kk in range(2):
                            k = 2 * (j % 8) + kk
                            part = modw[j % MRING][:, kk * 512:(kk + 1) * 512]
                            co = cv[:, 2 * KT + k:2 * KT + k + 1]
                            a = modacc[:, c % 2, :]
                            if k == 0:
                                w = nc.vector.tensor_scalar(a, part, co, None, ALU.mult)
                            else:
                                dve.wait_ge(mod_step, l * 2 * MU + 2 * j + kk)
                                w = nc.vector.scalar_tensor_tensor(a, part, co, a, ALU.mult, ALU.add)
                            w.then_inc(mod_step, 1)
                        dve.wait_ge(mod_step, l * 2 * MU + 2 * j + 2)
                        dve.sem_inc(mod_used, 1)
                    for w, nt in ((0, QLT), (1, KVT)):
                        r0 = QLT * w
                        own = rawlat[:, r0:r0 + nt, :]
                        s0 = LAT_AT[w]
                        if s == s0:
                            dve.wait_ge(lat[w]["raw"], l + 1)
                            tt(flat(sqlat[:, r0:r0 + nt, :]), flat(own), flat(own), ALU.mult).then_inc(lat[w]["sq"], 1)
                        if s == s0 + SUM_LAG:
                            dve.wait_ge(lat[w]["sum"], l + 1)
                            nc.vector.tensor_scalar(sc[:, LS + 2 * w:LS + 2 * w + 2], M[2 * w][:, 0:2], 1.0 / (nt * P), None,
                                                    ALU.mult).then_inc(lat[w]["ss"], 1)
                        if s == s0 + ROT_LAG:
                            dve.wait_ge(lat[w]["rstd"], l + 1)
                            for t in range(MT):
                                i = nc.vector.tensor_scalar(rot[:, t, :], ident[:, :], 0.0, sc[:, LR + 2 * w + t:LR + 2 * w + t + 1],
                                                            ALU.mult, ALU.add)
                            i.then_inc(lat[w]["rot"], 1)
                        if s == s0 + ROW_LAG:
                            dve.wait_ge(lat[w]["row"], l + 1)
                            for k in range(nt):
                                gain = gs[:, 2 * KT + r0 + k:2 * KT + r0 + k + 1]
                                i = nc.vector.scalar_tensor_tensor(own[:, k, :], own[:, k, :], gain, M[2 * w + 1][:, 0:SEQ],
                                                                   ALU.mult, ALU.mult)
                            i.then_inc(lat[w]["val"], 1)
                        if s == s0 + HI_LAG:
                            dve.wait_ge(lat[w]["hi"], l + 1)
                            hi, lo = ((qlh, qll), (kvh, kvl))[w]
                            tt(flat(lo[:, :, :]), flat(own), flat(hi[:, :, :]).bitcast(F32), ALU.subtract).then_inc(lat[w]["lo"], 1)
                    g = ENDED.get(s)
                    name = GROUPS[g][0] if g is not None else None
                    if name is not None:
                        a = acc[g % 2]
                        i = g - G_OF[name]
                        if g in DVE_READS:
                            dve.wait_ge(half_used, base + s + CREDIT)
                    if name in ("kvlat", "uq"):
                        n = 0 if name == "kvlat" else i + 1
                        dve.wait_ge(swap_in, 5 * l + n + 1)
                        if name == "kvlat":
                            tt(rtmp[:, :], rtmp[:, :], cosT[:, :], ALU.mult)
                        else:
                            tt(rtmp[:, :], a[:, 512:768], cosT[:, :], ALU.mult).then_inc(acc_dve, 1)
                        tt(swap[:, :], swap[:, :], sinT[:, :], ALU.mult).then_inc(rope_prod, 1)
                        dve.wait_ge(rope_prod, 5 * l + n + 1)
                        o = kpe[:, :] if name == "kvlat" else qpe[:, i, :]
                        tt(o, rtmp[:, :], swap[:, :], ALU.add).then_inc(rope_out, 1)
                        dve.wait_ge(rope_out, 5 * l + n + 1)
                    if name == "xin":
                        dve.wait_ge(acc_act, l * READS_ACT + 13)
                        nc.vector.memset(U[:, :, 0:1], 0.0)
                        nc.vector.memset(U[:, :, SEQ + 1:SEQ + 2], 0.0)
                        tt(U[:, :, 1:SEQ + 1], a[:, :].rearrange("p (t n) -> p t n", n=SEQ), O[:, HEADS:HEADS + CT, :],
                           ALU.mult).then_inc(acc_dve, 1)
                        dve.wait_ge(acc_dve, l * READS_DVE + 5)
                    for t in range(CT):
                        if s == H_AT[G_OF["xin"] + 1] + 1 + t:
                            o = O[:, HEADS + t, :]
                            for tap in range(3):
                                wt = gs[:, C_CONV + 3 * t + tap:C_CONV + 3 * t + tap + 1]
                                if tap == 0:
                                    w = nc.vector.tensor_scalar(o, U[:, t, 0:SEQ], wt, None, ALU.mult)
                                else:
                                    w = nc.vector.scalar_tensor_tensor(o, U[:, t, tap:tap + SEQ], wt, o, ALU.mult, ALU.add)
                                w.then_inc(conv_step, 1)
                                dve.wait_ge(conv_step, 12 * l + 3 * t + tap + 1)
                    if name == "gb":
                        own = O[:, HEADS:HEADS + CT, :]
                        tt(flat(own), a[:, :], flat(own), ALU.mult).then_inc(acc_dve, 1)
                        dve.wait_ge(acc_dve, l * READS_DVE + 6)
                    for i in range(4):
                        e = H_AT[G_OF["gate"] + i + 1]
                        n = l * 4 + i + 1
                        part = GATE_PART[i]
                        own = slice(4 * part, 4 * part + 4)
                        if s == e:
                            dve.wait_ge(g_tanh, n)
                            nc.vector.scalar_tensor_tensor(flat(gate[:, :, :]), flat(gate[:, :, :]), 1.0,
                                                           acc[(G_OF["gate"] + i) % 2][:, :], ALU.add, ALU.mult).then_inc(acc_dve, 1)
                        if s == e + 1:
                            dve.wait_ge(acc_dve, l * READS_DVE + 7 + i)
                            dve.wait_ge(o_out, l * NH + sum(q + PV_LAG <= e for q in QK_AT))
                            nc.vector.scalar_tensor_tensor(flat(gate[:, :, :]), flat(gate[:, :, :]), 0.5, flat(O[:, own, :]),
                                                           ALU.mult, ALU.mult).then_inc(y_val, 1)
                        if s == e + 2:
                            dve.wait_ge(y_hi, n)
                            tt(Ylo[:, own, :], gate[:, :, :], Yhi[:, own, :].bitcast(F32), ALU.subtract).then_inc(y_lo, 1)
                    for h in range(NH):
                        b = h % 2
                        n = l * NH + h + 1
                        if s == QK_AT[h]:
                            dve.wait_ge(S_ready, n)
                            nc.vector.tensor_reduce(sc[:, MX + 2 * b:MX + 2 * b + 2], M[b][:, :].rearrange("p (t n) -> p t n", t=MT),
                                                    AX_X, ALU.max).then_inc(mx_ready, 1)
                            dve.wait_ge(mx_ready, n)
                            nc.vector.tensor_scalar(sc[:, NM + 2 * b:NM + 2 * b + 2], sc[:, MX + 2 * b:MX + 2 * b + 2],
                                                    -float(QHEAD if h < HEADS else P) ** -0.5, None, ALU.mult).then_inc(nm_ready, 1)
                            dve.wait_ge(exp_ready, n)
                            nc.vector.reciprocal(sc[:, RINV + 2 * b:RINV + 2 * b + 2], sc[:, RSUM + 2 * b:RSUM + 2 * b + 2]).then_inc(inv_ready, 1)
                            dve.wait_ge(inv_ready, n)
                            for t in range(MT):
                                w = nc.vector.tensor_scalar(prob[:, b, t, :], prob[:, b, t, :],
                                                            sc[:, RINV + 2 * b + t:RINV + 2 * b + t + 1], None, ALU.mult)
                            w.then_inc(P_ready, 1)
                        if s == QK_AT[h] + PV_LAG:
                            dve.wait_ge(PV_done, n)
                            nc.vector.tensor_copy(O[:, h if h < HEADS else h + CT, :], M[3][:, 0:SEQ]).then_inc(o_out, 1)
                dve.wait_ge(acc_act, l * READS_ACT + READS_ACT)
                row_sums().then_inc(o_ss, 1)
                dve.wait_ge(post_in, 16 * l + 16)
                dve.wait_ge(o_rstd, l + 1)
                residual(post, l, l * 2)

            dve.wait_ge(mod_out, DEPTH * MCH)

            def mod(i):
                return modT[:, i * KT:(i + 1) * KT]

            def ng(i):
                return ngs[:, i * KT:(i + 1) * KT]

            def rr(i):
                return R[:, i * KT:(i + 1) * KT]

            nc.vector.scalar_tensor_tensor(rr(0), mod(1), 1.0, ng(0), ALU.add, ALU.mult)
            nc.vector.tensor_copy(rr(1), mod(0))
            tt(rr(2), mod(2), ng(1), ALU.mult)
            tt(rr(3), mod(5), ng(3), ALU.mult)
            nc.vector.scalar_tensor_tensor(A2[:, :], mod(4), 1.0, ng(2), ALU.add, ALU.mult).then_inc(r_ready, 1)
            dve.wait_ge(x_rstd, DEPTH + 1)
            dve.wait_ge(row_in[0], 16)
            for t in range(MT):
                nc.vector.scalar_tensor_tensor(xn[:, t, :], X[:, t, :], sc[:, RS + 2 + t:RS + 3 + t], rowb[0][:, :],
                                               ALU.mult, ALU.mult).then_inc(h_step, 1)
            dve.wait_ge(row_in[1], 16)
            for t in range(MT):
                dve.wait_ge(h_step, t + 1)
                w = tt(xn[:, t, :], xn[:, t, :], rowb[1][:, :], ALU.add)
            w.then_inc(h_ready, 1)
            for f in range(KT):
                dve.wait_ge(ab_act, f + 1)
                nc.vector.tensor_scalar(AB[:, f, SEQ:], M[f % 4][:, SEQ:], -1.0, None, ALU.mult).then_inc(ab_dve, 1)
            for s in range(AHEAD):
                split_lo(dve, FN_H, s, 1024)
            for f in range(KT):
                dve.wait_ge(f_hi, f + 1)
                tt(Hlo[:, f, :], M[f % 4][:, 0:SEQ], Hhi[:, f, :].bitcast(F32), ALU.subtract).then_inc(f_lo, 1)
            for s in range(AHEAD, 32):
                split_lo(dve, FN_H, s, 1024)
            dve.wait_ge(acc_act, ACT0 + 4)
            row_sums().then_inc(o_ss, 1)
            dve.wait_ge(row_in[2], 16)
            dve.wait_ge(o_rstd, DEPTH + 1)
            residual(rowb[2], DEPTH, DEPTH * 2)
            dve.wait_ge(x_rstd, DEPTH + 2)
            for t in range(MT):
                w = nc.vector.tensor_scalar(xn[:, t, :], X[:, t, :], sc[:, RS + 2 + t:RS + 3 + t], None, ALU.mult)
            w.then_inc(x_xn, 1)
            for f in range(KT):
                dve.wait_ge(x2_T, f + 1)
                if f >= 4:
                    dve.wait_ge(x2_lo, f - 3)
                nc.vector.tensor_scalar(vtmp[:, f % 4, :], M[f % 4][:, 0:SEQ], A2[:, f:f + 1], modT[:, 3 * KT + f:3 * KT + f + 1],
                                        ALU.mult, ALU.add).then_inc(x2_val, 1)
                if f:
                    dve.wait_ge(x2_hi, f)
                    tt(Hlo[:, f - 1, :], vtmp[:, (f - 1) % 4, :], Hhi[:, f - 1, :].bitcast(F32), ALU.subtract).then_inc(x2_lo, 1)
            dve.wait_ge(x2_hi, KT)
            dve.wait_ge(x2_val, KT)
            tt(Hlo[:, KT - 1, :], vtmp[:, (KT - 1) % 4, :], Hhi[:, KT - 1, :].bitcast(F32), ALU.subtract).then_inc(x2_lo, 1)
            nc.vector.memset(otok[:, :, :], 0.0).then_inc(acc_dve, 1)
            with dve.Fori(0, 4) as q:
                base = ML_H + 64 * q
                for s in range(AHEAD):
                    split_lo(dve, base, s, 1024)
                for s in range(65):
                    if s + AHEAD < 64:
                        split_lo(dve, base, s + AHEAD, 1024)
                    if s in (8, 16, 24, 32):
                        j = s // 8 - 1
                        n = 4 * q + j + 1
                        dve.wait_ge(m_rel, n)
                        tt(flat(sqr[:, :, :]), flat(rel[:, :, :]), flat(rel[:, :, :]), ALU.mult).then_inc(m_sq, 1)
                        dve.wait_ge(m_hi, n)
                        tt(Ylo[:, 4 * j:4 * j + 4, :], sqr[:, :, :], Yhi[:, 4 * j:4 * j + 4, :].bitcast(F32),
                           ALU.subtract).then_inc(m_lo, 1)
                        dve.wait_ge(m_lo, n)
                    if s in (40, 48, 56, 64):
                        j = s // 8 - 5
                        dve.wait_ge(half_used, base + s + CREDIT)
                        dve.wait_ge(acc_dve, DVE0 + 4 * q + 1)
                        part = otok[:, :, j * 512:(j + 1) * 512]
                        tt(part, acc[j % 2][:, :].rearrange("p (t n) -> p t n", t=MT), part, ALU.add).then_inc(acc_dve, 1)
            dve.wait_ge(row_in[3], 16)
            dve.wait_ge(o_rstd, DEPTH + 2)
            residual(rowb[3], DEPTH + 1, DEPTH * 2 + 2)

        @block.tensor
        def _(pe):
            pe.sem_inc(half_used, CREDIT)
            pe.wait_ge(ident_in, 16)
            pe.wait_ge(ones_set, 1)
            with pe.Fori(0, DEPTH) as l:
                base = l * LH

                def mod_sums_read(s):
                    c = sum(t <= s for t in MOD_T_AT)
                    if c:
                        pe.wait_ge(mod_out, l * MCH + c)

                pe.wait_ge(mem_xn, l + 1)
                for f in range(KT):
                    if f >= 4:
                        pe.wait_ge(mem_lo, l * KT + f - 3)
                    norm_T(memx, f).then_inc(mem_T, 1)
                for s in range(LH + 1):
                    if 6 <= s < 14:
                        if s == 6:
                            pe.wait_ge(x_xn, l + 1)
                            pe.wait_ge(mem_lo, l * KT + KT)
                        for f in (2 * (s - 6), 2 * (s - 6) + 1):
                            if f >= 4:
                                pe.wait_ge(x_lo, l * KT + f - 3)
                            if f % 4 == 3:
                                mod_sums_read(s)
                            norm_T(xn, f).then_inc(x_T, 1)
                    for w, nt in ((0, QLT), (1, KVT)):
                        s0 = LAT_AT[w]
                        if s == s0 + SUM_LAG:
                            pe.wait_ge(lat[w]["sq"], l + 1)
                            for t in range(MT):
                                for k in range(nt):
                                    i = mm(M[2 * w][:, t:t + 1], sqlat[:, QLT * w + k, t * P:(t + 1) * P], ones[:, 0:1], k == 0, k == nt - 1)
                            i.then_inc(lat[w]["sum"], 1)
                        if s == s0 + ROW_LAG:
                            pe.wait_ge(lat[w]["rot"], l + 1)
                            mod_sums_read(s)
                            for t in range(MT):
                                i = nc.tensor.transpose(M[2 * w + 1][:, t * P:(t + 1) * P], rot[:, t, :], ident[:, :])
                            i.then_inc(lat[w]["row"], 1)
                    for h in range(NH):
                        n = l * NH + h + 1
                        b = h % 2
                        mem_head = h - HEADS
                        if s == QK_AT[h] + PV_LAG:
                            pe.wait_ge(PT_out, n)
                            if h >= 1:
                                pe.wait_ge(o_out, n - 1)
                            mod_sums_read(s)
                            for kt in range(MT):
                                v = V[:, kt, h * VD:(h + 1) * VD] if h < HEADS else mv[:, kt, mem_head * P:(mem_head + 1) * P]
                                i = mm(M[3][:, 0:SEQ], v, probT[:, kt, :], kt == 0, kt == MT - 1)
                            i.then_inc(PV_done, 1)
                    for h in range(NH):
                        n = l * NH + h + 1
                        b = h % 2
                        if s == QK_AT[h] + PT_LAG:
                            pe.wait_ge(P_ready, n)
                            if h >= 1:
                                pe.wait_ge(PT_out, n - 1)
                            for kt in range(MT):
                                for t in range(MT):
                                    i = nc.tensor.transpose(M[2][:, kt * SEQ + t * P:kt * SEQ + (t + 1) * P],
                                                            prob[:, b, t, kt * P:(kt + 1) * P], ident[:, :])
                            i.then_inc(PT_done, 1)
                    for h in range(NH):
                        n = l * NH + h + 1
                        b = h % 2
                        mem_head = h - HEADS
                        if s == QK_AT[h]:
                            if h == 0:
                                pe.wait_ge(acc_act, l * READS_ACT + 13)
                                pe.wait_ge(rope_out, l * 5 + 5)
                                pe.wait_ge(lat[1]["lo"], l + 1)
                            if h == HEADS:
                                pe.wait_ge(acc_act, l * READS_ACT + 14)
                            if h >= 2:
                                pe.wait_ge(exp_ready, n - 2)
                            for t in range(MT):
                                tok = slice(t * P, (t + 1) * P)
                                o = M[b][:, t * SEQ:(t + 1) * SEQ]
                                if h < HEADS:
                                    pb = 64 * (h % 2)
                                    mm(o, O[:, h, tok], kn[:, h, :], True, False)
                                    i = mm(o, qpe[pb:pb + 64, h // 2, tok], kpe[pb:pb + 64, :], False, True)
                                else:
                                    i = mm(o, O[:, h + CT, tok], mkT[:, mem_head, :], True, True)
                            i.then_inc(S_ready, 1)
                    if s + 1 in MOD_T_AT:
                        c = MOD_T_AT.index(s + 1)
                        pe.wait_ge(mod_used, l * MU + 8 * c + 8 + MRING)
                        if c >= 1:
                            pe.wait_ge(mod_out, l * MCH + c)
                        if 6 <= s < H_AT[G_OF["qlat"]]:
                            pe.wait_ge(x_lo, l * KT + min(2 * (s - 5), KT))
                        if LAT_AT[1] + ROW_LAG <= s < QK_AT[0] + PV_LAG:
                            pe.wait_ge(lat[1]["val"], l + 1)
                        heads = sum(q + PV_LAG <= s for q in QK_AT)
                        if heads:
                            pe.wait_ge(o_out, l * NH + heads)
                        for t in range(4):
                            i = mm(M[3][:, MODCOL + t:MODCOL + t + 1], modacc[:, c % 2, t * P:(t + 1) * P], ones[:, 0:1], True, True)
                        i.then_inc(mod_T, 1)
                    if s == LH:
                        continue
                    g = group_of(s)
                    name, kind, width, units, nk = GROUPS[g]
                    first, last = s == H_AT[g], s == H_AT[g + 1] - 1
                    n = nk // 2
                    k0 = (s - H_AT[g]) * n
                    if first and g >= 2:
                        ra, rd = sum(r <= g - 2 for r in ACT_READS), sum(r <= g - 2 for r in DVE_READS)
                        pe.wait_ge(acc_act, l * READS_ACT + ra)
                        if g - 2 in DVE_READS:
                            pe.wait_ge(acc_dve, l * READS_DVE + rd)
                    if name == "mk":
                        pe.wait_ge(mem_lo, l * KT + k0 + n)
                    if name == "qlat":
                        pe.wait_ge(x_lo, l * KT + k0 + n)
                    if name == "uq" and first:
                        pe.wait_ge(lat[0]["lo"], l + 1)
                    if name == "ukv" and first:
                        pe.wait_ge(lat[1]["lo"], l + 1)
                    if name == "wo":
                        pe.wait_ge(y_lo, l * 4 + GATE_PART.index(k0 // 4) + 1)
                    pe.wait_ge(lo_ready, base + s + 1)
                    act_in = (Yhi, Ylo) if name in ("mk", "mv", "wo") else (Hhi, Hlo)
                    if kind == "FM":
                        w = fm_half(s, acc[g % 2], act_in, four[0:width // P], k0, n, first, last, width)
                    elif kind == "TM":
                        w = tm_half(s, acc[g % 2], act_in, k0, n, first, last, width)
                    elif kind == "UQ":
                        w = fm_half(s, acc[g % 2], (qlh, qll), four[0:3], k0, n, first, last, width)
                    else:
                        w = ukv_half(s, acc[g % 2], k0, first, last)
                    w.then_inc(half_used, 1)
            pe.wait_ge(r_ready, 1)
            nc.tensor.transpose(M[0][0:64, 0:P], R[:, :], ident[:, :]).then_inc(r_T, 1)
            pe.wait_ge(h_ready, 1)
            pe.wait_ge(dft_in, 16)
            for f in range(KT):
                if f >= 4:
                    pe.wait_ge(ab_dve, f - 3)
                for t in range(MT):
                    i = mm(M[f % 4][:, :], xn[:, t, f * P:(f + 1) * P], cs[:, t, :], t == 0, t == MT - 1)
                i.then_inc(ab_ps, 1)
            pe.wait_ge(ab_act, KT)
            pe.wait_ge(ab_dve, KT)
            for f in range(KT):
                if f >= 4:
                    pe.wait_ge(f_lo, f - 3)
                g, j = f // 2, f % 2
                o = M[f % 4][:, 0:SEQ]
                for i in range(2):
                    mm(o, cs[:, i, j * P:(j + 1) * P], AB[:, 2 * g + i, 0:SEQ], i == 0, False)
                    w = mm(o, cs[:, i, SEQ + j * P:SEQ + (j + 1) * P], AB[:, 2 * g + i, SEQ:], False, i == 1)
                w.then_inc(f_ps, 1)
            for s in range(32):
                n = s // 8
                if s % 8 == 0 and n >= 2:
                    pe.wait_ge(acc_act, ACT0 + n - 1)
                pe.wait_ge(f_lo, min(2 * s + 2, KT))
                pe.wait_ge(lo_ready, FN_H + s + 1)
                tm_half(s, acc[n % 2], (Hhi, Hlo), 2 * (s % 8), 2, s % 8 == 0, s % 8 == 7, 512).then_inc(half_used, 1)
            pe.wait_ge(x_xn, DEPTH + 1)
            for f in range(KT):
                if f >= 4:
                    pe.wait_ge(x2_val, f - 3)
                norm_T(xn, f).then_inc(x2_T, 1)
            with pe.Fori(0, 4) as q:
                base = ML_H + 64 * q
                for s in range(64):
                    n = s // 8
                    if s % 8 == 0 and n < 2:
                        pe.wait_ge(acc_dve, DVE0 + 4 * q + 1)
                    if s % 8 == 0 and 2 <= n < 6:
                        pe.wait_ge(m_rel, 4 * q + n - 1)
                    if s % 8 == 0 and n >= 6:
                        pe.wait_ge(acc_dve, DVE0 + 4 * q + n - 4)
                    if n < 1:
                        pe.wait_ge(x2_lo, 2 * s + 2)
                    if n == 4:
                        pe.wait_ge(m_lo, 4 * q + (s - 32) // 2 + 1)
                    pe.wait_ge(lo_ready, base + s + 1)
                    k0 = 2 * (s % 8)
                    if n < 4:
                        w = fm_half(s, acc[n % 2], (Hhi, Hlo), four, k0, 2, k0 == 0, k0 == 14, 512)
                    else:
                        w = tm_half(s, acc[n % 2], (Yhi, Ylo), k0, 2, k0 == 0, k0 == 14, 512)
                    w.then_inc(half_used, 1)


def kernel(**inputs):
    import numpy as np
    import concourse.bacc as bacc
    from concourse.bass_utils import run_bass_kernel_spmd

    a = {k: np.asarray(v) for k, v in inputs.items()}

    def fm(v):
        return np.ascontiguousarray(np.moveaxis(v.reshape(*v.shape[:-1], -1, P), -1, -2))

    pad = np.zeros((DEPTH, P, G_CONST - C_CONV - 3 * CT), np.float32)
    conv = np.moveaxis(a["conv_w"].reshape(DEPTH, 3, CT, P), (1, 2, 3), (3, 2, 1)).reshape(DEPTH, P, 3 * CT)
    small = np.concatenate([fm(a["pre_norm_g"]), fm(a["mem_norm_g"]), fm(a["q_norm_g"]), fm(a["kv_norm_g"]), conv, pad], axis=2)
    half = ROPE // 2
    freq = np.float32(1.0) / (10000.0 ** (np.arange(0, ROPE, 2) / ROPE)).astype(np.float32)
    sign = np.tile(np.repeat(np.array([-1.0, 1.0], np.float32), half), 2)
    rope_c = np.stack([np.tile(freq, P // half), sign], axis=1).astype(np.float32)
    turn = 2.0 * np.pi * (np.outer(np.arange(SEQ), np.arange(SEQ)) % SEQ) / SEQ
    dft = np.concatenate([np.cos(turn), np.sin(turn)], axis=1).astype(np.float32)
    uq = a["w_uq"].reshape(DEPTH, QL, HEADS // 2, 2, QHEAD)
    uq = np.concatenate([uq[..., :NOPE].reshape(DEPTH, QL, HEADS // 2, 2 * NOPE),
                         uq[..., NOPE:].reshape(DEPTH, QL, HEADS // 2, 2 * ROPE)], axis=3).reshape(DEPTH, QL, HEADS * QHEAD)
    arrays = {
        "x": a["x"][0], "mem": a["mem"][0], "positions": a["positions"].reshape(SEQ), "small": np.ascontiguousarray(small),
        "w_in": a["w_in"], "w_uq": uq, "w_ukv": a["w_ukv"], "w_mk": a["w_mk"], "w_mv": a["w_mv"], "w_o": a["w_o"],
        "post_g": a["post_norm_g"], "consts": np.eye(P, dtype=np.float32), "rope_c": rope_c, "dft": dft,
        "cvec": fm(a["c_2"][0]), "bmod": fm(a["b_mod_2"][0]),
        "ng2": np.ascontiguousarray(np.moveaxis(fm(a["norm_g_2"][0]), 0, 1).reshape(P, 4 * KT)),
        "w_mod": a["w_mod_2"][0], "w_fnet": a["fnet_w_out_2"][0], "w_mlp_in": a["w_mlp_in_2"][0], "w_mlp_out": a["w_mlp_out_2"][0],
    }
    arrays = {k: np.ascontiguousarray(v) for k, v in arrays.items()}
    nc = bacc.Bacc("TRN2", target_bir_lowering=False, num_devices=1)
    aps = {k: nc.dram_tensor(f"in_{k}", v.shape, mybir.dt.from_np(v.dtype), kind="ExternalInput").ap() for k, v in arrays.items()}
    out = nc.dram_tensor("out_0", [SEQ, D], F32, kind="ExternalOutput").ap()
    build_program(nc, **aps, out=out)
    r = run_bass_kernel_spmd(nc, [{f"in_{k}": v for k, v in arrays.items()}], core_ids=[0])
    return r.results[0]["out_0"].reshape(1, SEQ, D)
```

```python
from contextlib import ExitStack

import concourse.bass as bass
from concourse import mybir

F32 = mybir.dt.float32
F32R = mybir.dt.float32r
I32 = mybir.dt.int32
BF16 = mybir.dt.bfloat16
ALU = mybir.AluOpType
ACT = mybir.ActivationFunctionType
AX_X = mybir.AxisListType.X

P = 128
D = 2048
SEQ = 256
MT = SEQ // P
KT = D // P
DEPTH = 2
HEADS, NOPE, ROPE, VD = 8, 128, 64, 128
QHEAD = NOPE + ROPE
QL, KVL = 512, 256
QLT, KVT = QL // P, KVL // P
CW = 512
CT = CW // P
MH = 4
EPS = 1e-6
NMOD = 6
MODCOLS = NMOD * D

C_Q = 0
C_KV = C_Q + QL
C_GB = C_KV + KVL + ROPE
C_GC = C_GB + CW
C_XIN = C_GC + CW
C_QM = C_XIN + CW
C_GATE = C_QM + MH * P

UNITW = 2048
RAW = 4
HIR = 4
CREDIT = 8
AHEAD = 3
LO_POOL = 4

GROUPS = (
    [("mem", "MEM", 512, 8, 4), ("qlat", "FM", 512, 4, 4), ("kvlat", "FM", 384, 4, 4),
     ("gc", "FM", 512, 4, 4)]
    + [("uq", "UQ", 384, 1, 4)] * 4 + [("ukv", "UKV", 512, 1, 2)] * 4
    + [("xin", "FM", 512, 4, 4), ("gb", "FM", 512, 4, 4), ("qmem", "FM", 512, 4, 4)]
    + [("gate", "FM", 512, 4, 4)] * 4 + [("wo", "TM", 512, 4, 4)] * 4
)
NG = len(GROUPS)
UNIT_AT = [sum(g[3] for g in GROUPS[:i]) for i in range(NG + 1)]
LU = UNIT_AT[-1]
LH = 2 * LU
H_AT = [2 * u for u in UNIT_AT]
G_OF = {name: i for i, name in reversed(list(enumerate(g[0] for g in GROUPS)))}
assert LU % RAW == 0 and LH % HIR == 0 and NG % 2 == 1


def acc_of(g):
    return (g + 1) % 2


def group_of(s):
    return max(g for g in range(NG) if H_AT[g] <= s)


ACT_READS = [0, 0] + [g for g in range(1, NG) if GROUPS[g][0] not in ("xin", "gb")]
DVE_READS = [g for g in range(NG) if GROUPS[g][0] in ("uq", "xin", "gb", "gate", "wo")]
ACC_CREDIT = 2
MK_END = H_AT[1] - 2
READS_ACT, READS_DVE = len(ACT_READS), len(DVE_READS)

MCH = MODCOLS // 512 // DEPTH
MU = MCH * KT // 2
MRING = 3
MOD_LEAD = 4


def mod_unit(s):
    return MOD_AT.index(s) if s in MOD_AT else None


GATE_PART = (2, 0, 1, 3)

QK_AT = [59 + 3 * h for h in range(HEADS)] + [84 + 3 * h for h in range(MH)]
NH = HEADS + MH
PT_LAG, PV_LAG = 4, 6
SUM_LAG, ROT_LAG, ROW_LAG, HI_LAG = 2, 4, 7, 8
C_CONV = 2 * KT + QLT + KVT
G_CONST = C_CONV + 3 * CT + 10

X_AT = 0
X_T_AT = 9
LAT_AT = (H_AT[G_OF["gc"] - 1], H_AT[G_OF["gc"]] + 1)
MOD_PAUSE = [*range(H_AT[G_OF["uq"]], H_AT[G_OF["xin"]] + 2), LAT_AT[1] + SUM_LAG, H_AT[G_OF["wo"] + 1] - 1, H_AT[G_OF["wo"] + 2] - 1,
             *(h + 1 for h in H_AT[G_OF["gate"] + 1:G_OF["gate"] + 5])]
MOD_AT = [s for s in range(H_AT[1], LH - 6) if s not in MOD_PAUSE][:MU]
assert len(MOD_AT) == MU
M3_BUSY = [q + PV_LAG for q in QK_AT] + [LAT_AT[1] + ROW_LAG]
MOD_T_AT = [min(t for t in range(MOD_AT[8 * c + 7] + 6, LH) if t - 1 not in M3_BUSY and t not in M3_BUSY) for c in range(MCH)]
MEM_AT = {f: 4 * (f // 4 - 1) + f % 4 // 2 for f in range(4, KT)}
MEM_HEAD = {f: LH - 10 + 2 * f for f in range(4)}
ENDED = {H_AT[g + 1]: g for g in range(NG)}
PI = 3.1415925
INV_TURN = 0.15915494309189535
ROUNDER = 12582912.0
TURN_PARTS = (6.28125, 0.001934051513671875, 1.255422830581665e-06, 2.430840251310684e-10)


def half_of(s):
    g = GROUPS[group_of(s)]
    return g[2] * g[4] // 2


def build_program(nc, x, memt, positions, small, w_in, w_uq, w_ukv, w_mk, w_mv, w_o, post_g,
                  consts, rope_c, dft, cvec, bmod, ng2, w_mod, w_fnet, w_mlp_in, w_mlp_out, out):
    scratch = nc.dram_tensor("mod_rows", [2 * KT, P], F32).ap()
    ctx = ExitStack()
    with ctx:
        origin = nc.sbuf_base + (-nc.sbuf_base) % 64

        def at(name, shape, kb, dt=F32):
            return nc.alloc_sbuf_tensor_at(name, shape, dt, offset=origin + int(kb * 1024))

        def sem(name):
            return ctx.enter_context(nc.semaphore(name))

        Hhi = at("Hhi", [P, KT, SEQ], 0, F32R)
        Hlo = at("Hlo", [P, KT, SEQ], 16, F32R)
        Yhi = at("Yhi", [P, KT, SEQ], 32, F32R)
        Ylo = at("Ylo", [P, KT, SEQ], 48, F32R)
        raw = [at(f"raw{i}", [P, UNITW], 64 + 8 * i) for i in range(RAW)]
        wlo = [at(f"wlo{i}", [P, UNITW], 64 + 8 * i, F32R) for i in range(RAW)]
        whi = [at(f"whi{i}", [P, UNITW // 2], 96 + 4 * i, F32R) for i in range(HIR)]
        X = at("X", [P, MT, D], 112)
        A = 128
        qlh = at("qlh", [P, QLT, SEQ], A, F32R)
        qll = at("qll", [P, QLT, SEQ], A + 4, F32R)
        kvh = at("kvh", [P, KVT, SEQ], A + 8, F32R)
        kvl = at("kvl", [P, KVT, SEQ], A + 10, F32R)
        prob = at("prob", [P, 2, MT, SEQ], A)
        probT = at("probT", [P, MT, SEQ], A + 4)
        U = at("U", [P, CT, SEQ + 2], A + 6)
        junk = at("junk", [P, D], A, BF16)
        memr = at("memr", [P, 2, 4, SEQ], A + 4)
        rows = at("rows", [2 * KT, P], A + 10)
        O = at("O", [P, KT, SEQ], A + 12)
        qpe = at("qpe", [P, HEADS // 2, SEQ], A + 28)
        kn = at("kn", [P, HEADS, SEQ], A + 32)
        kpe = at("kpe", [P, SEQ], A + 40)
        V = at("V", [P, MT, HEADS * VD], A + 41)
        mkT = at("mkT", [P, MH, SEQ], A + 49)
        mv = at("mv", [P, MT, MH * P], A + 53)
        cosT = at("cosT", [P, SEQ], A + 57)
        sinT = at("sinT", [P, SEQ], A + 58)
        swap = at("swap", [P, SEQ], A + 59)
        mrow = at("mrow", [P, SEQ], A + 60)
        pos = at("pos", [P, SEQ], A + 49, I32)
        rot = at("rot", [P, MT, P], A + 59)
        rawlat = at("rawlat", [P, QLT + KVT, SEQ], A + 32)
        sqlat = at("sqlat", [P, QLT + KVT, SEQ], A + 41)
        memx = at("memx", [P, KT, SEQ], 48)
        msq = at("msq", [P, KT, SEQ], 32)
        xn = at("xn", [P, MT, D], A + 12)
        csx = at("csx", [P, MT, 2 * SEQ], A + 12)
        xrot = at("xrot", [P, MT, P], A + 4)
        otok = at("otok", [P, MT, D], A + 12)
        memh = at("memh", [P, 8, SEQ], A + 28, F32R)
        meml = at("meml", [P, 8, SEQ], A + 36, F32R)
        post = at("post", [P, D], A + 44)
        gate = at("gate", [P, CT, SEQ], A + 6)
        AB = at("AB", [P, KT, SEQ], 32)
        pq = at("pq", [P, 2, 2, SEQ], 48)
        mix = at("mix", [P, 2, 2, SEQ], 52)
        rowb = [at(f"rowb{i}", [P, D], A + 44 + 8 * i) for i in range(2)]
        rel = at("rel", [P, CT, SEQ], A + 28)
        sqr = at("sqr", [P, CT, SEQ], A + 32)
        vtmp = at("vtmp", [P, 4, SEQ], A + 36)
        fin = at("fin", [P, MT, D], A + 36)
        modw = [at(f"modw{i}", [P, 1024], A + 61 + 4 * i) for i in range(MRING)]
        cs = at("cs", [P, MT, 2 * SEQ], A + 61)
        modacc = at("modacc", [P, 2, 512], A + 73)
        m = A + 77
        ident = at("ident", [P, P], m)
        ones = at("ones", [P, 8], m + 0.5)
        gs = at("gs", [P, G_CONST], m + 0.5625)
        modT = at("modT", [P, NMOD * KT], m + 0.8125)
        ngs = at("ngs", [P, 4 * KT], m + 1.1875)
        R = at("R", [P, 2 * KT], m + 1.4375)
        A1 = at("A1", [P, KT], m + 1.5625)
        S1 = at("S1", [P, KT], m + 1.625)
        A2 = at("A2", [P, KT], m + 1.6875)
        cv = at("cv", [P, 3 * KT], m + 1.75)
        ropev = at("ropev", [P, 2], m + 1.9375)
        sc = at("sc", [P, 64], m + 1.96875)
        SS, MS, RS = 0, 4, 8
        LS, LM, LR = 12, 16, 20
        NM, RSUM, RINV = 24, 28, 32
        PS = 36
        OS, OM, OR = 44, 46, 48
        POW, EPSC, MX = 50, 52, 54
        modS = at("modS", [P, 4 * MCH], m + 2.25)
        assert origin + (m + 2.4375) * 1024 <= nc.sbuf_top

        acc = [ctx.enter_context(nc.psum_tensor(f"acc{i}", [P, 1024], F32)) for i in range(2)]
        M = [ctx.enter_context(nc.psum_tensor(f"M{i}", [P, 512], F32)) for i in range(4)]
        MODCOL = 480

        raw_in = [sem(f"raw_in{i}") for i in range(RAW)]
        hi_ready, lo_ready = sem("hi_ready"), sem("lo_ready")
        half_used = sem("half_used")
        acc_act, acc_dve = sem("acc_act"), sem("acc_dve")
        ident_in, x_in, small_in, post_in = map(sem, ("ident_in", "x_in", "small_in", "post_in"))
        mem_in = [sem(f"mem_in{i}") for i in range(4)]
        memr_in = [sem(f"memr_in{i}") for i in range(2)]
        vec_in, rope_in, c_in, dft_in = map(sem, ("vec_in", "rope_in", "c_in", "dft_in"))
        ones_set, pow_set = sem("ones_set"), sem("pow_set")
        rope_step, ang_ready, sin_ready, c_exp = map(sem, ("rope_step", "ang_ready", "sin_ready", "c_exp"))
        lo_pool = sem("lo_pool")
        sq_step, pool_step = sem("sq_step"), sem("pool_step")
        mem_sq, mem_add, mem_sum, mem_ss, mem_rstd, mem_rot, mem_T, mem_row, mem_xn, mem_hi, mem_lo = map(sem, (
            "mem_sq", "mem_add", "mem_sum", "mem_ss", "mem_rstd", "mem_rot", "mem_T", "mem_row", "mem_xn", "mem_hi", "mem_lo"))
        x_ss, x_rstd, x_xn, x_T, x_hi, x_lo = map(sem, ("x_ss", "x_rstd", "x_xn", "x_T", "x_hi", "x_lo"))
        residual_done = sem("residual_done")
        LN = ("raw", "sq", "sum", "ss", "rstd", "rot", "row", "val", "hi", "lo")
        lat = [{n: sem(f"{w}_{n}") for n in LN} for w in ("q", "kv")]
        swap_in, rope_prod, rope_out, conv_step = map(sem, ("swap_in", "rope_prod", "rope_out", "conv_step"))
        S_ready, mx_ready, nm_ready, exp_ready, inv_ready, P_ready, PT_done, PT_out, PV_done, o_out = map(sem, (
            "S_ready", "mx_ready", "nm_ready", "exp_ready", "inv_ready", "P_ready", "PT_done", "PT_out", "PV_done", "o_out"))
        g_tanh, y_val, y_hi, y_lo = map(sem, ("g_tanh", "y_val", "y_hi", "y_lo"))
        row_sq, o_ss, o_rstd, x_new, zero_set = map(sem, ("row_sq", "o_ss", "o_rstd", "x_new", "zero_set"))
        mod_in = [sem(f"mod_in{i}") for i in range(MRING)]
        mod_used, mod_step, mod_T, mod_out, mod_done = map(sem, ("mod_used", "mod_step", "mod_T", "mod_out", "mod_done"))
        r_ready, r_T, rows_ready, rows_out = map(sem, ("r_ready", "r_T", "rows_ready", "rows_out"))
        row_in = [sem(f"row_in{i}") for i in range(2)]
        csx_ready, ab_ps, ab_out, ab_val, f_ps, f_pq, f_mix, f_hi, f_lo = map(sem, (
            "csx_ready", "ab_ps", "ab_out", "ab_val", "f_ps", "f_pq", "f_mix", "f_hi", "f_lo"))
        x2_T, x2_rot, x2_row, x2_rowed, x2_val, x2_shifted, x2_hi, x2_lo, x2_lo_pool = map(sem, ("x2_T", "x2_rot", "x2_row", "x2_rowed", "x2_val", "x2_shifted", "x2_hi", "x2_lo", "x2_lo_pool"))
        m_rel, m_sq, m_hi, m_lo = map(sem, ("m_rel", "m_sq", "m_hi", "m_lo"))
        fin_step = sem("fin_step")
        stored = sem("stored")

        FN_H, ML_H = DEPTH * LH, DEPTH * LH + 32
        LO0 = DEPTH * (LH - LH // LO_POOL)
        ACT0 = DEPTH * READS_ACT + ACC_CREDIT
        DVE0 = DEPTH * READS_DVE + ACC_CREDIT
        DVE1 = DVE0 + 4

        def load_unit(sp, base, u, dst, src):
            sp.wait_ge(half_used, base + 2 * (u - RAW) + 2 + CREDIT)
            sp.dma_start(dst, src).then_inc(raw_in[u % RAW], 16)

        def weight_rows(w, k0, nk, c0, n):
            return w[k0 * P:(k0 + nk) * P, c0:c0 + n].rearrange("(k p) n -> p k n", p=P)

        def slot(u, nk, n):
            return raw[u % RAW][:, 0:nk * n].rearrange("p (k n) -> p k n", k=nk)

        def split_hi(act, base, s, n):
            u = s // 2
            act.wait_ge(raw_in[u % RAW], 2 * base + 16 * (u // RAW + 1))
            act.wait_ge(half_used, base + s - HIR + 1 + CREDIT)
            nc.scalar.activation(whi[s % HIR][:, 0:n], raw[u % RAW][:, (s % 2) * n:(s % 2) * n + n],
                                 ACT.Copy).then_inc(hi_ready, 1)

        def split_lo(engine, unit, base, s, n, done):
            u = s // 2
            engine.wait_ge(hi_ready, base + s + 1)
            part = slice((s % 2) * n, (s % 2) * n + n)
            unit.tensor_tensor(wlo[u % RAW][:, part], raw[u % RAW][:, part],
                               whi[s % HIR][:, 0:n].bitcast(F32), ALU.subtract).then_inc(done, 1)

        def of_pool(s):
            return s % LO_POOL == LO_POOL - 1

        def mm(o, a, b, start, stop):
            return nc.tensor.matmul(o, a, b, start=start, stop=stop, skip_group_check=True)

        def halves(s, width, nk):
            n = nk * width
            hi = whi[s % HIR][:, 0:n].rearrange("p (k n) -> p k n", n=width)
            lo = wlo[s // 2 % RAW][:, (s % 2) * n:(s % 2) * n + n].rearrange("p (k n) -> p k n", n=width)
            return hi, lo

        def fm_half(s, ps, act_in, cols, k0, nk, first, last, width):
            hi, lo = halves(s, width, nk)
            ah, al = act_in
            for kk in range(nk):
                k = k0 + kk
                for t, col in enumerate(cols):
                    o = ps[:, t * SEQ:(t + 1) * SEQ]
                    mm(o, col(hi[:, kk, :]), ah[:, k, :], first and kk == 0 and t % 2 == 0, False)
                    mm(o, col(hi[:, kk, :]), al[:, k, :], False, False)
                    w = mm(o, col(lo[:, kk, :]), ah[:, k, :], False, last and kk == nk - 1)
            return w

        def tm_half(s, ps, act_in, k0, nk, first, last, width):
            hi, lo = halves(s, width, nk)
            ah, al = act_in
            for kk in range(nk):
                k = k0 + kk
                for t in range(MT):
                    o = ps[:, t * width:(t + 1) * width]
                    tok = slice(t * P, (t + 1) * P)
                    mm(o, ah[:, k, tok], hi[:, kk, :], first and kk == 0, False)
                    mm(o, ah[:, k, tok], lo[:, kk, :], False, False)
                    w = mm(o, al[:, k, tok], hi[:, kk, :], False, last and kk == nk - 1)
            return w

        def ukv_half(s, ps, k, first, last):
            hi, lo = halves(s, 512, 1)
            fm_half(s, ps, (kvh, kvl), [lambda w: w[:, 0:NOPE], lambda w: w[:, 256:256 + NOPE]], k, 1, first, last, 512)

            def vcols(w):
                return w[:, 0, :].rearrange("p (h c) -> p h c", h=2)[:, :, NOPE:NOPE + VD]

            for t in range(MT):
                o = ps[:, 512 + t * SEQ:512 + (t + 1) * SEQ].rearrange("p (h c) -> p h c", h=2)
                tok = slice(t * P, (t + 1) * P)
                mm(o, kvh[:, k, tok], vcols(hi), first and t == 0, False)
                mm(o, kvh[:, k, tok], vcols(lo), False, False)
                w = mm(o, kvl[:, k, tok], vcols(hi), False, last)
            return w

        four = [lambda w, t=t: w[:, t * P:(t + 1) * P] for t in range(4)]

        def bank(g):
            return acc[g // 2][:, g % 2 * 512:(g % 2 + 1) * 512] if g < 4 else M[g - 4][:, :]

        block = ctx.enter_context(nc.Block())

        @block.sync
        def _(sp):
            for b in range(4):
                sp.dma_start(memx[:, 4 * b:4 * b + 4, :], memt[4 * b:4 * b + 4].rearrange("k p n -> p k n")).then_inc(mem_in[b], 16)
            sp.dma_start(gs[:, :], small[0]).then_inc(small_in, 16)
            with sp.Fori(0, DEPTH) as l:
                def load_mem(b):
                    sp.dma_start(memr[:, b % 2, :, :], memt[4 * b:4 * b + 4].rearrange("k p n -> p k n")).then_inc(memr_in[b % 2], 16)

                def of_layer(w):
                    return w[bass.ds(l, 1)].rearrange("a k n -> (a k) n")

                w_mod_l = w_mod.rearrange("k (l n) -> l k n", l=DEPTH)[bass.ds(l, 1)].rearrange("a k n -> (a k) n")

                def load_mods(u):
                    for s in (2 * u - MOD_LEAD, 2 * u - MOD_LEAD + 1):
                        j = mod_unit(s)
                        if j is not None:
                            sp.wait_ge(mod_used, l * MU + j + 1)
                            sp.dma_start(modw[j % MRING][:, :].rearrange("p (k n) -> p k n", k=2),
                                         weight_rows(w_mod_l, 2 * (j % 8), 2, 512 * (j // 8), 512)).then_inc(mod_in[j % MRING], 16)

                w_in_l = of_layer(w_in)
                mem_w = (of_layer(w_mk), of_layer(w_mv))
                src = {"mem": (None, 0), "qlat": (w_in_l, C_Q), "kvlat": (w_in_l, C_KV),
                       "gc": (w_in_l, C_GC), "uq": (of_layer(w_uq), 0), "ukv": (of_layer(w_ukv), 0), "xin": (w_in_l, C_XIN),
                       "gb": (w_in_l, C_GB), "qmem": (w_in_l, C_QM), "gate": (w_in_l, C_GATE), "wo": (of_layer(w_o), 0)}
                for g, (name, kind, width, units, nk) in enumerate(GROUPS):
                    w, c0 = src[name]
                    for i in range(units):
                        u = UNIT_AT[g] + i
                        if kind == "MEM":
                            load_unit(sp, l * LH, u, slot(u, nk, width), weight_rows(mem_w[i % 2], i // 2 * nk, nk, 0, width))
                            for b in (2, 3):
                                if u == 2 * b - 2:
                                    sp.wait_ge(mem_lo, l * KT + 4 * (b - 1))
                                    load_mem(b)
                            load_mods(u)
                            continue
                        if name == "gate":
                            c0 = C_GATE + (GATE_PART[g - G_OF[name]] - (g - G_OF[name])) * width
                        load_unit(sp, l * LH, u, slot(u, nk, width),
                                  weight_rows(w, i * nk, nk, c0 + (g - G_OF[name]) * width, width))
                        load_mods(u)
                    if g == G_OF["wo"] - 1:
                        sp.wait_ge(o_out, l * NH + NH)
                        sp.wait_ge(conv_step, 12 * l + 12)
                        sp.dma_start(gs[:, :], small[bass.ds(l + 1, 1), :, :].rearrange("a p n -> p (a n)")).then_inc(small_in, 16)
                        sp.dma_start(post[:, :], post_g[bass.ds(l, 1), :].partition_broadcast(P)).then_inc(post_in, 16)
                    if g == G_OF["wo"] + 1:
                        sp.wait_ge(y_lo, l * 4 + 4)
                        load_mem(0)
                        load_mem(1)
            for i in range(4):
                load_unit(sp, FN_H, i, slot(i, 4, 512), weight_rows(w_fnet, 4 * i, 4, 0, 512))
            sp.wait_ge(mod_used, DEPTH * MU + MRING)
            sp.dma_start(cs[:, :, :], dft.rearrange("(t p) n -> p t n", p=P)).then_inc(dft_in, 16)
            sp.wait_ge(rows_ready, 1)
            sp.dma_start(scratch, rows[:, :]).then_inc(rows_out, 16)
            sp.wait_ge(rows_out, 16)
            sp.wait_ge(residual_done, 2 * DEPTH + 2)
            for i in range(2):
                row = scratch[i * KT:(i + 1) * KT, :].rearrange("k p -> (k p)")
                sp.dma_start(rowb[i][:, :], row.partition_broadcast(P)).then_inc(row_in[i], 16)
            for n in range(1, 4):
                for i in range(4):
                    u = 4 * n + i
                    load_unit(sp, FN_H, u, slot(u, 4, 512), weight_rows(w_fnet, 4 * i, 4, 512 * n, 512))
            with sp.Fori(0, 4) as q:
                w1 = w_mlp_in.rearrange("k (q n) -> q k n", q=4)[bass.ds(q, 1)].rearrange("a k n -> (a k) n")
                w2 = w_mlp_out.rearrange("(q k) n -> q k n", q=4)[bass.ds(q, 1)].rearrange("a k n -> (a k) n")
                for n in range(8):
                    for i in range(4):
                        u = 4 * n + i
                        load_unit(sp, ML_H + 64 * q, u, slot(u, 4, 512),
                                  weight_rows(w1 if n < 4 else w2, 4 * i, 4, 512 * (n % 4), 512))
            for i in range(2 * MT):
                sp.wait_ge(x_new, 2 * DEPTH + 4 + i + 1)
                t, c = i // 2, slice(i % 2 * (D // 2), (i % 2 + 1) * (D // 2))
                sp.dma_start(out[t * P:(t + 1) * P, c], X[:, t, c]).then_inc(stored, 16)
            sp.wait_ge(stored, 32 * MT)

        @block.gpsimd
        def _(pool):
            nc.gpsimd.memset(ones[:, :], 1.0).then_inc(ones_set, 1)
            nc.gpsimd.memset(sc[:, POW:POW + 2], -0.5).then_inc(pow_set, 1)
            nc.gpsimd.memset(sc[:, EPSC:EPSC + 2], EPS).then_inc(pow_set, 1)
            nc.gpsimd.memset(otok[:, :, :], 0.0).then_inc(zero_set, 1)
            pool.wait_ge(pow_set, 2)

            def rstd(s0, m0, r0, step, done, n=2):
                nc.gpsimd.tensor_tensor(sc[:, m0:m0 + n], sc[:, s0:s0 + n], sc[:, EPSC:EPSC + n], ALU.add).then_inc(pool_step, 1)
                pool.wait_ge(pool_step, step)
                nc.gpsimd.tensor_tensor(sc[:, r0:r0 + n], sc[:, m0:m0 + n], sc[:, POW:POW + n], ALU.pow).then_inc(done, 1)

            pool.wait_ge(mem_ss, 1)
            rstd(SS, MS, RS, 1, mem_rstd)
            pool.wait_ge(mem_row, 1)
            for f in range(8):
                nc.gpsimd.tensor_tensor(memr[:, f // 4, f % 4, :], memx[:, f, :], mrow[:, :], ALU.mult).then_inc(mem_xn, 1)
            with pool.Fori(0, DEPTH) as l:
                def norm_mem(b, n):
                    pool.wait_ge(memr_in[b % 2], 32 * l + 16 * n)
                    for i in range(4):
                        own = memr[:, b % 2, i, :]
                        nc.gpsimd.tensor_tensor(own, own, mrow[:, :], ALU.mult).then_inc(mem_xn, 1)

                for s in range(LH):
                    if s == 0:
                        pool.wait_ge(o_ss, l + 1)
                        rstd(OS, OM, OR, l * 4 + 2, o_rstd)
                    if of_pool(s + AHEAD):
                        split_lo(pool, nc.gpsimd, l * LH, s + AHEAD, half_of(s + AHEAD), lo_pool)
                    if s == 0:
                        norm_mem(2, 1)
                    if s == X_AT + 3:
                        pool.wait_ge(x_ss, l + 1)
                        rstd(SS + 2, MS + 2, RS + 2, l * 4 + 3, x_rstd)
                    if s == 4:
                        norm_mem(3, 1)
                    for i in range(2):
                        if s == LAT_AT[i] + SUM_LAG + 1:
                            pool.wait_ge(lat[i]["ss"], l + 1)
                            rstd(LS + 2 * i, LM + 2 * i, LR + 2 * i, l * 4 + 4 + i, lat[i]["rstd"])
                    if s == MEM_HEAD[0] - 4:
                        norm_mem(0, 2)
                        norm_mem(1, 2)
            n = DEPTH * 4 + 1
            pool.wait_ge(o_ss, DEPTH + 1)
            rstd(OS, OM, OR, n + 1, o_rstd)
            for t in range(MT):
                pool.wait_ge(sq_step, 2 * DEPTH + t + 2)
                rstd(SS + 2 + t, MS + 2 + t, RS + 2 + t, n + 2 + t, x_rstd, 1)
            pool.wait_ge(o_ss, DEPTH + 2)
            rstd(OS, OM, OR, n + 4, o_rstd)
            pool.wait_ge(x_ss, DEPTH + 2)
            rstd(SS + 2, MS + 2, RS + 2, n + 5, x_rstd)
            for f in range(1, KT, 2):
                pool.wait_ge(x2_hi, f + 1)
                nc.gpsimd.tensor_tensor(Hlo[:, f, :], vtmp[:, f % 4, :], Hhi[:, f, :].bitcast(F32), ALU.subtract).then_inc(x2_lo_pool, 1)
            pool.wait_ge(x_new, 2 * DEPTH + 4)
            nc.gpsimd.memset(otok[:, :, :], 0.0).then_inc(zero_set, 1)
            pool.wait_ge(o_ss, DEPTH + 3)
            rstd(OS, OM, OR, n + 6, o_rstd)

        @block.scalar
        def _(act):
            def squares(src, c, at_step, done, ready=None, ready_at=0):
                for t in range(MT):
                    act.wait_ge(sq_step, at_step + t + 1)
                    if ready is not None:
                        act.wait_ge(ready, ready_at + t + 1)
                    w = nc.scalar.activation(junk[:, :], src[:, t, :], ACT.Square, scale=D ** -0.5, accum_out=sc[:, c + t:c + t + 1])
                    w.then_inc(sq_step, 1)
                act.wait_ge(sq_step, at_step + MT + 1)
                act.sem_inc(done, 1)

            def flat(ap):
                return ap.rearrange("p h n -> p (h n)")

            def row_squares(tiles, n):
                for t in range(MT):
                    q = junk[:, t * 512 + 1024 * (n % 2):(t + 1) * 512 + 1024 * (n % 2)]
                    w = nc.scalar.activation(q, tiles[t], ACT.Square, scale=D ** -0.5,
                                             accum_out=sc[:, PS + 4 * t + n:PS + 4 * t + n + 1])
                    w.then_inc(row_sq, 1)

            def round_mem(base, of_layer, f):
                act.wait_ge(mem_xn, of_layer + f + 1)
                if f >= 8:
                    act.wait_ge(half_used, base + 4 * (f // 4 - 2) + 3 + f % 4 // 2 + CREDIT)
                nc.scalar.activation(memh[:, f % 8, :], memr[:, f // 4 % 2, f % 4, :], ACT.Copy,
                                     scale=gs[:, KT + f:KT + f + 1]).then_inc(mem_hi, 1)

            act.dma_start(ropev[:, :], rope_c).then_inc(rope_in, 16)
            act.dma_start(pos[:, :], positions.partition_broadcast(P)).then_inc(rope_in, 16)
            act.dma_start(ident[:, :], consts).then_inc(ident_in, 16)
            act.dma_start(cv[:, 0:KT], cvec).then_inc(c_in, 16)
            act.dma_start(modT[:, :], bmod).then_inc(vec_in, 16)
            act.dma_start(ngs[:, :], ng2).then_inc(vec_in, 16)
            act.sem_inc(sq_step, 1)
            for b in range(4):
                act.wait_ge(mem_in[b], 16)
                four_tiles = slice(4 * b, 4 * b + 4)
                nc.scalar.activation(flat(msq[:, four_tiles, :]), flat(memx[:, four_tiles, :]), ACT.Square).then_inc(mem_sq, 1)
            act.dma_start(X[:, :, :], x.rearrange("(t p) d -> p t d", p=P)).then_inc(x_in, 16)
            act.sem_inc(acc_act, ACC_CREDIT)
            for s in range(AHEAD):
                split_hi(act, 0, s, 1024)
            act.wait_ge(mem_T, 1)
            nc.scalar.activation(mrow[:, :], M[1][:, 0:SEQ], ACT.Copy).then_inc(mem_row, 1)
            act.wait_ge(small_in, 16)
            for f in range(4):
                round_mem(0, 0, f)
            act.wait_ge(ang_ready, 1)
            nc.scalar.activation(swap[:, :], sinT[:, :], ACT.Sin).then_inc(sin_ready, 1)
            nc.scalar.activation(kpe[:, :], cosT[:, :], ACT.Sin).then_inc(sin_ready, 1)
            act.wait_ge(c_in, 16)
            nc.scalar.activation(cv[:, KT:2 * KT], cv[:, 0:KT], ACT.Exp, scale=-1.0).then_inc(c_exp, 1)

            with act.Fori(0, DEPTH) as l:
                base = l * LH

                for s in range(LH + 1):
                    if s < LH:
                        split_hi(act, base, s + AHEAD, half_of((s + AHEAD) % LH))
                    if s in MOD_T_AT:
                        c = MOD_T_AT.index(s)
                        if c == 0:
                            act.wait_ge(mod_done, l)
                        act.wait_ge(mod_T, l * MCH + c + 1)
                        nc.scalar.activation(modS[:, 4 * c:4 * c + 4], M[3][:, MODCOL:MODCOL + 4], ACT.Copy).then_inc(mod_out, 1)
                    for h in range(NH):
                        b = h % 2
                        if s == QK_AT[h]:
                            act.wait_ge(nm_ready, l * NH + h + 1)
                            scale = float(QHEAD if h < HEADS else P) ** -0.5
                            for t in range(MT):
                                w = nc.scalar.activation(prob[:, b, t, :], M[b][:, t * SEQ:(t + 1) * SEQ], ACT.Exp, scale=scale,
                                                         bias=sc[:, NM + 2 * b + t:NM + 2 * b + t + 1],
                                                         accum_out=sc[:, RSUM + 2 * b + t:RSUM + 2 * b + t + 1])
                            w.then_inc(exp_ready, 1)
                        if s == QK_AT[h] + PT_LAG:
                            act.wait_ge(PT_done, l * NH + h + 1)
                            nc.scalar.activation(flat(probT[:, :, :]), M[2][:, :], ACT.Copy).then_inc(PT_out, 1)
                        if s == QK_AT[h] + PV_LAG:
                            act.wait_ge(PV_done, l * NH + h + 1)
                            nc.scalar.activation(O[:, h if h < HEADS else h + CT, :], M[3][:, 0:SEQ], ACT.Copy).then_inc(o_out, 1)
                    for f in MEM_AT:
                        if s == MEM_AT[f]:
                            round_mem(base, l * KT, f)
                    for f in MEM_HEAD:
                        if s == MEM_HEAD[f]:
                            act.wait_ge(small_in, 16 * l + 32)
                            round_mem(base, l * KT + KT, f)
                    if s == X_AT + 2:
                        squares(X, SS + 2, l * 2, x_ss, x_new, l * 2)
                    if X_T_AT <= s < X_T_AT + KT // 2:
                        for f in (2 * (s - X_T_AT), 2 * (s - X_T_AT) + 1):
                            act.wait_ge(x_T, l * KT + f + 1)
                            nc.scalar.activation(Hhi[:, f, :], M[f % 4][:, 0:SEQ], ACT.Copy,
                                                 scale=gs[:, f:f + 1]).then_inc(x_hi, 1)
                    for w, nt in ((0, QLT), (1, KVT)):
                        if s == LAT_AT[w] + HI_LAG:
                            act.wait_ge(lat[w]["val"], l + 1)
                            o, i = (qlh, 0) if w == 0 else (kvh, QLT)
                            nc.scalar.activation(flat(o[:, :, :]), flat(rawlat[:, i:i + nt, :]), ACT.Copy).then_inc(lat[w]["hi"], 1)
                    g = ENDED.get(s)
                    name = GROUPS[g][0] if g is not None else None
                    if name is not None:
                        a = acc[acc_of(g)]
                        i = g - G_OF[name]
                        act.wait_ge(half_used, base + s + CREDIT)
                    if s == MK_END:
                        act.wait_ge(half_used, base + s + CREDIT)
                        nc.scalar.activation(flat(mkT[:, :, :]), acc[0][:, :], ACT.Copy).then_inc(acc_act, 1)
                    if name == "mem":
                        nc.scalar.activation(flat(mv[:, :, :]), acc[1][:, :], ACT.Copy).then_inc(acc_act, 1)
                    if name == "qlat":
                        nc.scalar.activation(flat(rawlat[:, 0:QLT, :]), a[:, :], ACT.Copy).then_inc(lat[0]["raw"], 1)
                        nc.scalar.activation(flat(sqlat[:, 0:QLT, :]), a[:, :], ACT.Square).then_inc(lat[0]["sq"], 1)
                        act.wait_ge(lat[0]["sq"], l + 1)
                        act.sem_inc(acc_act, 1)
                    if name == "kvlat":
                        nc.scalar.activation(flat(rawlat[:, QLT:, :]), a[:, 0:512], ACT.Copy).then_inc(lat[1]["raw"], 1)
                        nc.scalar.activation(flat(sqlat[:, QLT:, :]), a[:, 0:512], ACT.Square).then_inc(lat[1]["sq"], 1)
                        for b in range(4):
                            h = 32 * (b % 2)
                            nc.scalar.activation(kpe[32 * b:32 * b + 32, :], a[h:h + 32, 512:768], ACT.Copy)
                            w = nc.scalar.activation(swap[32 * b:32 * b + 32, :], a[32 - h:64 - h, 512:768], ACT.Copy)
                        w.then_inc(swap_in, 1)
                        act.wait_ge(swap_in, 5 * l + 1)
                        act.sem_inc(acc_act, 1)
                    if name == "gc":
                        nc.scalar.activation(flat(O[:, HEADS:HEADS + CT, :]), a[:, :], ACT.Copy).then_inc(acc_act, 1)
                    if name == "uq":
                        act.wait_ge(rope_out, l * 5 + i + 1)
                        for b in range(4):
                            w = nc.scalar.activation(swap[32 * b:32 * b + 32, :], a[32 * (b ^ 1):32 * (b ^ 1) + 32, 512:768], ACT.Copy)
                        w.then_inc(swap_in, 1)
                        nc.scalar.activation(flat(O[:, 2 * i:2 * i + 2, :]), a[:, 0:512], ACT.Copy).then_inc(acc_act, 1)
                    if name == "ukv":
                        nc.scalar.activation(V[:, :, 256 * i:256 * i + 256],
                                             a[:, 512:1024].rearrange("p (t n) -> p t n", t=MT), ACT.Copy)
                        nc.scalar.activation(flat(kn[:, 2 * i:2 * i + 2, :]), a[:, 0:512], ACT.Copy).then_inc(acc_act, 1)
                    if name == "qmem":
                        nc.scalar.activation(flat(O[:, HEADS + CT:, :]), a[:, :], ACT.Copy).then_inc(acc_act, 1)
                    if name == "gate":
                        if i:
                            act.wait_ge(y_lo, l * 4 + i)
                        nc.scalar.activation(flat(gate[:, :, :]), a[:, :], ACT.Tanh, scale=0.5).then_inc(g_tanh, 1)
                        act.wait_ge(g_tanh, l * 4 + i + 1)
                        act.sem_inc(acc_act, 1)
                    if name == "wo":
                        row_squares([a[:, t * 512:(t + 1) * 512] for t in range(MT)], i)
                        act.wait_ge(row_sq, 2 * (4 * l + i) + 2)
                        act.sem_inc(acc_act, 1)
                    for i in range(4):
                        if s == H_AT[G_OF["gate"] + i + 1] + 2:
                            act.wait_ge(y_val, l * 4 + i + 1)
                            part = GATE_PART[i]
                            nc.scalar.activation(Yhi[:, 4 * part:4 * part + 4, :], gate[:, :, :], ACT.Copy).then_inc(y_hi, 1)
                    for h in range(NH):
                        b = h % 2
                        if s == QK_AT[h] + 1:
                            act.wait_ge(inv_ready, l * NH + h + 1)
                            for t in range(MT):
                                w = nc.scalar.activation(prob[:, b, t, :], prob[:, b, t, :], ACT.Copy,
                                                         scale=sc[:, RINV + 2 * b + t:RINV + 2 * b + t + 1])
                            w.then_inc(P_ready, 1)
            act.wait_ge(r_T, 1)
            nc.scalar.activation(rows[:, :], M[0][0:2 * KT, 0:P], ACT.Copy).then_inc(rows_ready, 1)
            squares(X, SS + 2, DEPTH * 2, x_ss, x_new, DEPTH * 2)
            for g in range(KT // 2):
                act.wait_ge(ab_ps, g + 1)
                for f in (2 * g, 2 * g + 1):
                    w = nc.scalar.activation(AB[:, f, :], bank(g)[:, f % 2 * SEQ:(f % 2 + 1) * SEQ], ACT.Copy, scale=A1[:, f:f + 1])
                w.then_inc(ab_out, 1)
            for g in range(KT // 2 + 2):
                if g < KT // 2:
                    act.wait_ge(f_ps, g + 1)
                    if g >= 2:
                        act.wait_ge(f_mix, g - 1)
                    nc.scalar.activation(flat(pq[:, g % 2, :, :]), bank(g), ACT.Copy).then_inc(f_pq, 1)
                if g >= 2:
                    act.wait_ge(f_mix, g - 1)
                    nc.scalar.activation(Hhi[:, 2 * g - 4:2 * g - 2, :], mix[:, g % 2, :, :], ACT.Copy).then_inc(f_hi, 1)
            for s in range(33):
                if s < 32:
                    split_hi(act, FN_H, s + AHEAD, 1024)
                if s and s % 8 == 0:
                    act.wait_ge(half_used, FN_H + s + CREDIT)
                    row_squares([acc[(s // 8 - 1) % 2][:, t * 512:(t + 1) * 512] for t in range(MT)], s // 8 - 1)
                    act.wait_ge(row_sq, 2 * (4 * DEPTH + s // 8 - 1) + 2)
                    act.sem_inc(acc_act, 1)
            squares(X, SS + 2, 2 + DEPTH * 2, x_ss, x_new, DEPTH * 2 + 2)
            act.wait_ge(x2_row, 1)
            nc.scalar.activation(mrow[:, :], M[3][:, SEQ:], ACT.Copy).then_inc(x2_rowed, 1)
            for f in range(KT):
                act.wait_ge(x2_val, f + 1)
                shift = modT[:, 3 * KT + f:3 * KT + f + 1]
                if f % 2 == 0:
                    nc.scalar.activation(Hhi[:, f, :], vtmp[:, f % 4, :], ACT.Identity, bias=shift).then_inc(x2_hi, 1)
                else:
                    nc.scalar.activation(vtmp[:, f % 4, :], vtmp[:, f % 4, :], ACT.Identity, bias=shift).then_inc(x2_shifted, 1)
                    act.wait_ge(x2_shifted, f // 2 + 1)
                    nc.scalar.activation(Hhi[:, f, :], vtmp[:, f % 4, :], ACT.Copy).then_inc(x2_hi, 1)

            def mlp_round(q, ahead):
                base = ML_H + 64 * q
                for s in range(64):
                    if s + AHEAD < ahead:
                        split_hi(act, base, s + AHEAD, 1024)
                    if ahead == 64 and s in (41, 49, 57):
                        whole_squares(s // 8 - 5)
                    if s in (8, 16, 24, 32):
                        j = s // 8 - 1
                        act.wait_ge(half_used, base + s + CREDIT)
                        nc.scalar.activation(flat(rel[:, :, :]), acc[j % 2][:, :], ACT.Relu).then_inc(m_rel, 1)
                        act.wait_ge(m_sq, 4 * q + j + 1)
                        nc.scalar.activation(Yhi[:, 4 * j:4 * j + 4, :], sqr[:, :, :], ACT.Copy).then_inc(m_hi, 1)

            def whole_squares(j):
                act.wait_ge(acc_dve, DVE1 + 12 + j + 1)
                row_squares([otok[:, t, j * 512:(j + 1) * 512] for t in range(MT)], j)

            with act.Fori(0, 3) as q:
                mlp_round(q, 64 + AHEAD)
            mlp_round(3, 64)
            whole_squares(3)

        @block.vector
        def _(dve):
            def flat(ap):
                return ap.rearrange("p h n -> p (h n)")

            def tt(o, a, b, op):
                return nc.vector.tensor_tensor(o, a, b, op)

            def step(ins, n):
                ins.then_inc(rope_step, 1)
                dve.wait_ge(rope_step, n)

            dve.wait_ge(rope_in, 32)
            step(nc.vector.tensor_copy(kpe[:, :], pos[:, :]), 1)
            step(nc.vector.tensor_scalar(sinT[:, :], kpe[:, :], ropev[:, 0:1], None, ALU.mult), 2)
            step(nc.vector.tensor_scalar(cosT[:, :], sinT[:, :], INV_TURN, ROUNDER, ALU.mult, ALU.add), 3)
            step(nc.vector.tensor_scalar(cosT[:, :], cosT[:, :], ROUNDER, None, ALU.subtract), 4)
            for i, part in enumerate(TURN_PARTS):
                step(nc.vector.scalar_tensor_tensor(sinT[:, :], cosT[:, :], -part, sinT[:, :], ALU.mult, ALU.add), 5 + i)
            n = 5 + len(TURN_PARTS)
            step(nc.vector.tensor_scalar(sinT[:, :], sinT[:, :], -PI, PI, ALU.max, ALU.min), n)
            nc.vector.tensor_scalar(cosT[:, :], sinT[:, :], 0.5, None, ALU.mult).then_inc(ang_ready, 1)
            for i in range(3):
                dve.wait_ge(mem_sq, i + 2)
                if i:
                    dve.wait_ge(mem_add, i)
                tt(flat(msq[:, 0:4, :]), flat(msq[:, 0:4, :]), flat(msq[:, 4 * i + 4:4 * i + 8, :]), ALU.add).then_inc(mem_add, 1)
            for i, half in ((3, 2), (4, 1)):
                dve.wait_ge(mem_add, i)
                tt(flat(msq[:, 0:half, :]), flat(msq[:, 0:half, :]), flat(msq[:, half:2 * half, :]), ALU.add).then_inc(mem_add, 1)
            split_lo(dve, nc.vector, 0, 0, 1024, lo_ready)
            dve.wait_ge(mem_sum, 1)
            nc.vector.tensor_scalar(sc[:, SS:SS + 2], M[0][:, 0:2], 1.0 / D, None, ALU.mult).then_inc(mem_ss, 1)
            split_lo(dve, nc.vector, 0, 1, 1024, lo_ready)
            dve.wait_ge(mem_rstd, 1)
            dve.wait_ge(ident_in, 16)
            for t in range(MT):
                w = nc.vector.tensor_scalar(rot[:, t, :], ident[:, :], 0.0, sc[:, RS + t:RS + t + 1], ALU.mult, ALU.add)
            w.then_inc(mem_rot, 1)
            dve.sem_inc(mod_used, MRING)
            dve.sem_inc(acc_dve, ACC_CREDIT)
            split_lo(dve, nc.vector, 0, 2, 1024, lo_ready)

            def residual(src, n):
                for t in range(MT):
                    nc.vector.scalar_tensor_tensor(X[:, t, :], src[t], sc[:, OR + t:OR + t + 1], X[:, t, :],
                                                   ALU.mult, ALU.add).then_inc(x_new, 1)
                for t in range(MT):
                    dve.wait_ge(x_new, 2 * n + t + 1)
                    dve.sem_inc(residual_done, 1)

            rows_of = [otok[:, t, :] for t in range(MT)]

            def scaled_rows(a, gain, n, squared):
                for t in range(MT):
                    dve.wait_ge(row_sq, squared + t + 1)
                    w = tt(otok[:, t, n * 512:(n + 1) * 512], a[:, t * 512:(t + 1) * 512], gain[:, n * 512:(n + 1) * 512], ALU.mult)
                return w

            def row_sums():
                return nc.vector.tensor_reduce(sc[:, OS:OS + 2], sc[:, PS:PS + 8].rearrange("p (t n) -> p t n", t=MT), AX_X, ALU.add)

            def mem_rest(of_layer, f):
                dve.wait_ge(mem_hi, of_layer + f + 1)
                nc.vector.scalar_tensor_tensor(meml[:, f % 8, :], memr[:, f // 4 % 2, f % 4, :], gs[:, KT + f:KT + f + 1],
                                               memh[:, f % 8, :].bitcast(F32), ALU.mult, ALU.subtract).then_inc(mem_lo, 1)

            for f in range(4):
                mem_rest(0, f)
            dve.wait_ge(sin_ready, 2)
            nc.vector.tensor_scalar(sinT[:, :], swap[:, :], ropev[:, 1:2], None, ALU.mult)
            step(tt(cosT[:, :], kpe[:, :], kpe[:, :], ALU.mult), n + 1)
            step(nc.vector.tensor_scalar(cosT[:, :], cosT[:, :], -2.0, 1.0, ALU.mult, ALU.add), n + 2)
            dve.wait_ge(c_exp, 1)
            step(nc.vector.tensor_scalar(cv[:, KT:2 * KT], cv[:, KT:2 * KT], 1.0, None, ALU.add), n + 3)
            step(nc.vector.reciprocal(cv[:, 2 * KT:], cv[:, KT:2 * KT]), n + 4)
            step(tt(cv[:, 2 * KT:], cv[:, 2 * KT:], cv[:, 0:KT], ALU.mult), n + 5)
            nc.vector.memset(sc[:, PS:PS + 8], 0.0).then_inc(zero_set, 1)
            dve.wait_ge(zero_set, 2)
            dve.wait_ge(vec_in, 32)
            dve.wait_ge(x_in, 16)

            with dve.Fori(0, DEPTH) as l:
                base = l * LH

                dve.wait_ge(acc_act, l * READS_ACT + ACC_CREDIT)
                row_sums().then_inc(o_ss, 1)
                for s in range(LH + 1):
                    if s < LH and not of_pool(s + AHEAD):
                        split_lo(dve, nc.vector, base, s + AHEAD, half_of((s + AHEAD) % LH), lo_ready)
                    for h in range(NH):
                        b = h % 2
                        n = l * NH + h + 1
                        if s == QK_AT[h]:
                            dve.wait_ge(S_ready, n)
                            nc.vector.tensor_reduce(sc[:, MX + 2 * b:MX + 2 * b + 2], M[b][:, :].rearrange("p (t n) -> p t n", t=MT),
                                                    AX_X, ALU.max).then_inc(mx_ready, 1)
                            dve.wait_ge(mx_ready, n)
                            nc.vector.tensor_scalar(sc[:, NM + 2 * b:NM + 2 * b + 2], sc[:, MX + 2 * b:MX + 2 * b + 2],
                                                    -float(QHEAD if h < HEADS else P) ** -0.5, None, ALU.mult).then_inc(nm_ready, 1)
                        if s == QK_AT[h] + 1:
                            dve.wait_ge(exp_ready, n)
                            nc.vector.reciprocal(sc[:, RINV + 2 * b:RINV + 2 * b + 2], sc[:, RSUM + 2 * b:RSUM + 2 * b + 2]).then_inc(inv_ready, 1)

                    if s == X_AT:
                        dve.wait_ge(o_rstd, l + 1)
                        dve.wait_ge(acc_dve, l * READS_DVE + ACC_CREDIT)
                        residual(rows_of, l)
                    for f in MEM_AT:
                        if s == MEM_AT[f]:
                            mem_rest(l * KT, f)
                    for f in MEM_HEAD:
                        if s == MEM_HEAD[f]:
                            mem_rest(l * KT + KT, f)
                    for t in range(MT):
                        if s == X_AT + 5 + t:
                            dve.wait_ge(x_rstd, l + 1)
                            nc.vector.tensor_scalar(xn[:, t, :], X[:, t, :], sc[:, RS + 2 + t:RS + 3 + t], None, ALU.mult).then_inc(x_xn, 1)
                    if s == MOD_T_AT[-1] + 1:
                        dve.wait_ge(mod_out, l * MCH + MCH)
                        cols = modT[:, bass.ds(l * 4 * MCH, 4 * MCH)]
                        tt(cols, modS[:, :], cols, ALU.add).then_inc(mod_done, 1)
                    if X_T_AT <= s < X_T_AT + KT // 2:
                        for f in (2 * (s - X_T_AT), 2 * (s - X_T_AT) + 1):
                            dve.wait_ge(x_hi, l * KT + f + 1)
                            nc.vector.scalar_tensor_tensor(Hlo[:, f, :], M[f % 4][:, 0:SEQ], gs[:, f:f + 1],
                                                           Hhi[:, f, :].bitcast(F32), ALU.mult, ALU.subtract).then_inc(x_lo, 1)
                    j = mod_unit(s)
                    if j is not None:
                        c = j // 8
                        dve.wait_ge(mod_in[j % MRING], MU // MRING * 16 * l + 16 * (j // MRING + 1))
                        if j % 8 == 0 and c >= 2:
                            dve.wait_ge(mod_T, l * MCH + c - 1)
                        for kk in range(2):
                            k = 2 * (j % 8) + kk
                            part = modw[j % MRING][:, kk * 512:(kk + 1) * 512]
                            co = cv[:, 2 * KT + k:2 * KT + k + 1]
                            a = modacc[:, c % 2, :]
                            if k == 0:
                                w = nc.vector.tensor_scalar(a, part, co, None, ALU.mult)
                            else:
                                dve.wait_ge(mod_step, l * 2 * MU + 2 * j + kk)
                                w = nc.vector.scalar_tensor_tensor(a, part, co, a, ALU.mult, ALU.add)
                            w.then_inc(mod_step, 1)
                        dve.wait_ge(mod_step, l * 2 * MU + 2 * j + 2)
                        dve.sem_inc(mod_used, 1)
                    for w, nt in ((0, QLT), (1, KVT)):
                        r0 = QLT * w
                        own = rawlat[:, r0:r0 + nt, :]
                        s0 = LAT_AT[w]
                        if s == s0 + SUM_LAG:
                            dve.wait_ge(lat[w]["sum"], l + 1)
                            nc.vector.tensor_scalar(sc[:, LS + 2 * w:LS + 2 * w + 2], M[2 * w][:, 0:2], 1.0 / (nt * P), None,
                                                    ALU.mult).then_inc(lat[w]["ss"], 1)
                        if s == s0 + ROT_LAG:
                            dve.wait_ge(lat[w]["rstd"], l + 1)
                            for t in range(MT):
                                i = nc.vector.tensor_scalar(rot[:, t, :], ident[:, :], 0.0, sc[:, LR + 2 * w + t:LR + 2 * w + t + 1],
                                                            ALU.mult, ALU.add)
                            i.then_inc(lat[w]["rot"], 1)
                        if s == s0 + ROW_LAG:
                            dve.wait_ge(lat[w]["raw"], l + 1)
                            dve.wait_ge(lat[w]["row"], l + 1)
                            for k in range(nt):
                                gain = gs[:, 2 * KT + r0 + k:2 * KT + r0 + k + 1]
                                i = nc.vector.scalar_tensor_tensor(own[:, k, :], own[:, k, :], gain, M[2 * w + 1][:, 0:SEQ],
                                                                   ALU.mult, ALU.mult)
                            i.then_inc(lat[w]["val"], 1)
                        if s == s0 + HI_LAG:
                            dve.wait_ge(lat[w]["hi"], l + 1)
                            hi, lo = ((qlh, qll), (kvh, kvl))[w]
                            tt(flat(lo[:, :, :]), flat(own), flat(hi[:, :, :]).bitcast(F32), ALU.subtract).then_inc(lat[w]["lo"], 1)
                    g = ENDED.get(s)
                    name = GROUPS[g][0] if g is not None else None
                    if name is not None:
                        a = acc[acc_of(g)]
                        i = g - G_OF[name]
                        if g in DVE_READS:
                            dve.wait_ge(half_used, base + s + CREDIT)
                    if name in ("kvlat", "uq"):
                        n = 0 if name == "kvlat" else i + 1
                        dve.wait_ge(swap_in, 5 * l + n + 1)
                        if name == "kvlat":
                            o = kpe[:, :]
                            tt(o, o, cosT[:, :], ALU.mult)
                        else:
                            o = qpe[:, i, :]
                            tt(o, a[:, 512:768], cosT[:, :], ALU.mult).then_inc(acc_dve, 1)
                        tt(swap[:, :], swap[:, :], sinT[:, :], ALU.mult).then_inc(rope_prod, 1)
                        dve.wait_ge(rope_prod, 5 * l + n + 1)
                        tt(o, o, swap[:, :], ALU.add).then_inc(rope_out, 1)
                        dve.wait_ge(rope_out, 5 * l + n + 1)
                    if name == "xin":
                        dve.wait_ge(acc_act, l * READS_ACT + 5 + ACC_CREDIT)
                        nc.vector.memset(U[:, :, 0:1], 0.0)
                        nc.vector.memset(U[:, :, SEQ + 1:SEQ + 2], 0.0)
                        tt(U[:, :, 1:SEQ + 1], a[:, :].rearrange("p (t n) -> p t n", n=SEQ), O[:, HEADS:HEADS + CT, :],
                           ALU.mult).then_inc(acc_dve, 1)
                        dve.wait_ge(acc_dve, l * READS_DVE + 5 + ACC_CREDIT)
                    for t in range(CT):
                        if s == H_AT[G_OF["xin"] + 1] + 1 + t:
                            o = O[:, HEADS + t, :]
                            for tap in range(3):
                                wt = gs[:, C_CONV + 3 * t + tap:C_CONV + 3 * t + tap + 1]
                                if tap == 0:
                                    w = nc.vector.tensor_scalar(o, U[:, t, 0:SEQ], wt, None, ALU.mult)
                                else:
                                    w = nc.vector.scalar_tensor_tensor(o, U[:, t, tap:tap + SEQ], wt, o, ALU.mult, ALU.add)
                                w.then_inc(conv_step, 1)
                                dve.wait_ge(conv_step, 12 * l + 3 * t + tap + 1)
                    if name == "gb":
                        own = O[:, HEADS:HEADS + CT, :]
                        tt(flat(own), a[:, :], flat(own), ALU.mult).then_inc(acc_dve, 1)
                        dve.wait_ge(acc_dve, l * READS_DVE + 6 + ACC_CREDIT)
                    for i in range(4):
                        e = H_AT[G_OF["gate"] + i + 1]
                        n = l * 4 + i + 1
                        part = GATE_PART[i]
                        own = slice(4 * part, 4 * part + 4)
                        if s == e:
                            dve.wait_ge(g_tanh, n)
                            nc.vector.scalar_tensor_tensor(flat(gate[:, :, :]), flat(gate[:, :, :]), 1.0,
                                                           acc[acc_of(G_OF["gate"] + i)][:, :], ALU.add, ALU.mult).then_inc(acc_dve, 1)
                        if s == e + 1:
                            dve.wait_ge(acc_dve, l * READS_DVE + 7 + i + ACC_CREDIT)
                            dve.wait_ge(o_out, l * NH + sum(q + PV_LAG <= e for q in QK_AT))
                            nc.vector.scalar_tensor_tensor(flat(gate[:, :, :]), flat(gate[:, :, :]), 0.5, flat(O[:, own, :]),
                                                           ALU.mult, ALU.mult).then_inc(y_val, 1)
                        if s == e + 2:
                            dve.wait_ge(y_hi, n)
                            tt(Ylo[:, own, :], gate[:, :, :], Yhi[:, own, :].bitcast(F32), ALU.subtract).then_inc(y_lo, 1)
                    if name == "wo":
                        dve.wait_ge(post_in, 16 * l + 16)
                        scaled_rows(a, post, g - G_OF[name], 2 * (4 * l + g - G_OF[name])).then_inc(acc_dve, 1)
            dve.wait_ge(acc_act, ACT0)
            row_sums().then_inc(o_ss, 1)
            dve.wait_ge(mod_done, DEPTH)

            def mod(i):
                return modT[:, i * KT:(i + 1) * KT]

            def ng(i):
                return ngs[:, i * KT:(i + 1) * KT]

            tt(R[:, 0:KT], mod(2), ng(1), ALU.mult)
            tt(R[:, KT:], mod(5), ng(3), ALU.mult).then_inc(r_ready, 1)
            nc.vector.scalar_tensor_tensor(A1[:, :], mod(1), 1.0, ng(0), ALU.add, ALU.mult)
            nc.vector.tensor_scalar(S1[:, :], mod(0), float(SEQ), None, ALU.mult)
            nc.vector.scalar_tensor_tensor(A2[:, :], mod(4), 1.0, ng(2), ALU.add, ALU.mult)
            dve.wait_ge(o_rstd, DEPTH + 1)
            dve.wait_ge(acc_dve, DVE0)
            residual(rows_of, DEPTH)
            dve.wait_ge(dft_in, 16)
            for t in range(MT):
                dve.wait_ge(x_rstd, DEPTH + t + 1)
                nc.vector.tensor_scalar(csx[:, t, :], cs[:, t, :], sc[:, RS + 2 + t:RS + 3 + t], None, ALU.mult).then_inc(csx_ready, 1)
            for g in range(KT // 2):
                dve.wait_ge(ab_out, g + 1)
                tt(AB[:, 2 * g:2 * g + 2, 0], AB[:, 2 * g:2 * g + 2, 0], S1[:, 2 * g:2 * g + 2], ALU.add).then_inc(ab_val, 1)
            for g in range(KT // 2 + 2):
                if g >= 2:
                    dve.wait_ge(f_hi, g - 1)
                    tt(Hlo[:, 2 * g - 4:2 * g - 2, :], mix[:, g % 2, :, :], Hhi[:, 2 * g - 4:2 * g - 2, :].bitcast(F32),
                       ALU.subtract).then_inc(f_lo, 1)
                if g < KT // 2:
                    if g >= 2:
                        dve.wait_ge(f_lo, g - 1)
                    dve.wait_ge(f_pq, g + 1)
                    pair, both = mix[:, g % 2, :, :], pq[:, g % 2, :, :]
                    even, odd = both[:, :, 1:P], both[:, :, P + 1:]
                    nc.vector.tensor_copy(pair[:, :, 0:P + 1:P], both[:, :, 0:P + 1:P])
                    tt(pair[:, :, 1:P], even, odd, ALU.subtract)
                    tt(pair[:, :, SEQ - 1:P:-1], even, odd, ALU.add).then_inc(f_mix, 1)
            for s in range(33):
                if s < 32:
                    split_lo(dve, nc.vector, FN_H, s + AHEAD, 1024, lo_ready)
                if s and s % 8 == 0:
                    i = s // 8 - 1
                    if i == 0:
                        dve.wait_ge(row_in[0], 16)
                    scaled_rows(acc[i % 2], rowb[0], i, 2 * (4 * DEPTH + i)).then_inc(acc_dve, 1)
            row_sums().then_inc(o_ss, 1)
            dve.wait_ge(o_rstd, DEPTH + 2)
            dve.wait_ge(acc_dve, DVE0 + 4)
            residual(rows_of, DEPTH + 1)
            dve.wait_ge(x_rstd, DEPTH + 3)
            for t in range(MT):
                w = nc.vector.tensor_scalar(xrot[:, t, :], ident[:, :], 0.0, sc[:, RS + 2 + t:RS + 3 + t], ALU.mult, ALU.add)
            w.then_inc(x2_rot, 1)
            dve.wait_ge(x2_rowed, 1)

            def x2_rest(f):
                dve.wait_ge(x2_hi, f + 1)
                nc.vector.scalar_tensor_tensor(Hlo[:, f, :], vtmp[:, f % 4, :], modT[:, 3 * KT + f:3 * KT + f + 1],
                                               Hhi[:, f, :].bitcast(F32), ALU.add, ALU.subtract).then_inc(x2_lo, 1)

            for f in range(KT):
                if f in (0, KT - 2):
                    dve.wait_ge(x2_T, 1 if f == 0 else 2)
                if f >= 4:
                    dve.wait_ge(x2_lo_pool if f % 2 else x2_lo, f // 2 - 1)
                nc.vector.scalar_tensor_tensor(vtmp[:, f % 4, :], bank(f // 2)[:, f % 2 * SEQ:(f % 2 + 1) * SEQ], A2[:, f:f + 1],
                                               mrow[:, :], ALU.mult, ALU.mult).then_inc(x2_val, 1)
                if f % 2:
                    x2_rest(f - 1)

            def mlp_round(q, ahead):
                base = ML_H + 64 * q
                for s in range(65):
                    if s < 64 and s + AHEAD < ahead:
                        split_lo(dve, nc.vector, base, s + AHEAD, 1024, lo_ready)
                    if ahead == 64 and s in (42, 50, 58):
                        final_gain(s // 8 - 5)
                    if s in (8, 16, 24, 32):
                        j = s // 8 - 1
                        n = 4 * q + j + 1
                        dve.wait_ge(m_rel, n)
                        tt(flat(sqr[:, :, :]), flat(rel[:, :, :]), flat(rel[:, :, :]), ALU.mult).then_inc(m_sq, 1)
                        dve.wait_ge(m_hi, n)
                        tt(Ylo[:, 4 * j:4 * j + 4, :], sqr[:, :, :], Yhi[:, 4 * j:4 * j + 4, :].bitcast(F32),
                           ALU.subtract).then_inc(m_lo, 1)
                    if s in (40, 48, 56, 64):
                        j = s // 8 - 5
                        dve.wait_ge(half_used, base + s + CREDIT)
                        dve.wait_ge(zero_set, 3)
                        dve.wait_ge(acc_dve, DVE1 + 4 * q)
                        part = otok[:, :, j * 512:(j + 1) * 512]
                        tt(part, acc[j % 2][:, :].rearrange("p (t n) -> p t n", t=MT), part, ALU.add).then_inc(acc_dve, 1)

            def final_gain(j):
                if j == 0:
                    dve.wait_ge(row_in[1], 16)
                dve.wait_ge(acc_dve, DVE1 + 12 + j + 1)
                for t in range(MT):
                    c = slice(j * 512, (j + 1) * 512)
                    w = tt(fin[:, t, c], otok[:, t, c], rowb[1][:, c], ALU.mult)
                w.then_inc(fin_step, 1)

            with dve.Fori(0, 3) as q:
                mlp_round(q, 64 + AHEAD)
            mlp_round(3, 64)
            final_gain(3)
            dve.wait_ge(row_sq, 2 * (4 * DEPTH + 4 + 4))
            row_sums().then_inc(o_ss, 1)
            dve.wait_ge(fin_step, 4)
            dve.wait_ge(o_rstd, DEPTH + 3)
            for t in range(MT):
                for c in (slice(0, D // 2), slice(D // 2, D)):
                    nc.vector.scalar_tensor_tensor(X[:, t, c], fin[:, t, c], sc[:, OR + t:OR + t + 1], X[:, t, c],
                                                   ALU.mult, ALU.add).then_inc(x_new, 1)

        @block.tensor
        def _(pe):
            pe.sem_inc(half_used, CREDIT)
            pe.wait_ge(ident_in, 16)
            pe.wait_ge(ones_set, 1)
            pe.wait_ge(mem_add, 5)
            for t in range(MT):
                i = mm(M[0][:, t:t + 1], msq[:, 0, t * P:(t + 1) * P], ones[:, 0:1], True, True)
            i.then_inc(mem_sum, 1)
            pe.wait_ge(mem_rot, 1)
            for t in range(MT):
                i = nc.tensor.transpose(M[1][:, t * P:(t + 1) * P], rot[:, t, :], ident[:, :])
            i.then_inc(mem_T, 1)
            with pe.Fori(0, DEPTH) as l:
                base = l * LH

                def mod_sums_read(s):
                    c = sum(t <= s for t in MOD_T_AT)
                    if c:
                        pe.wait_ge(mod_out, l * MCH + c)

                def wait_lo(s):
                    if of_pool(s):
                        pe.wait_ge(lo_pool, l * (LH // LO_POOL) + s // LO_POOL + 1)
                    else:
                        pe.wait_ge(lo_ready, l * (LH - LH // LO_POOL) + s + 1 - (s + 1) // LO_POOL)

                for s in range(LH + 1):
                    if X_T_AT <= s < X_T_AT + KT // 2:
                        if s == X_T_AT:
                            pe.wait_ge(x_xn, 2 * l + 2)
                            pe.wait_ge(mem_row, 1)
                        for f in (2 * (s - X_T_AT), 2 * (s - X_T_AT) + 1):
                            if f >= 4:
                                pe.wait_ge(x_lo, l * KT + f - 3)
                            for t in range(MT):
                                i = nc.tensor.transpose(M[f % 4][:, t * P:(t + 1) * P], xn[:, t, f * P:(f + 1) * P], ident[:, :])
                            i.then_inc(x_T, 1)
                    for w, nt in ((0, QLT), (1, KVT)):
                        s0 = LAT_AT[w]
                        if s == s0 + SUM_LAG:
                            pe.wait_ge(lat[w]["sq"], l + 1)
                            for t in range(MT):
                                for k in range(nt):
                                    i = mm(M[2 * w][:, t:t + 1], sqlat[:, QLT * w + k, t * P:(t + 1) * P], ones[:, 0:1], k == 0, k == nt - 1)
                            i.then_inc(lat[w]["sum"], 1)
                        if s == s0 + ROW_LAG:
                            pe.wait_ge(lat[w]["rot"], l + 1)
                            mod_sums_read(s)
                            for t in range(MT):
                                i = nc.tensor.transpose(M[2 * w + 1][:, t * P:(t + 1) * P], rot[:, t, :], ident[:, :])
                            i.then_inc(lat[w]["row"], 1)
                    for h in range(NH):
                        n = l * NH + h + 1
                        b = h % 2
                        mem_head = h - HEADS
                        if s == QK_AT[h] + PV_LAG:
                            pe.wait_ge(PT_out, n)
                            if h >= 1:
                                pe.wait_ge(o_out, n - 1)
                            mod_sums_read(s)
                            for kt in range(MT):
                                v = V[:, kt, h * VD:(h + 1) * VD] if h < HEADS else mv[:, kt, mem_head * P:(mem_head + 1) * P]
                                i = mm(M[3][:, 0:SEQ], v, probT[:, kt, :], kt == 0, kt == MT - 1)
                            i.then_inc(PV_done, 1)
                    for h in range(NH):
                        n = l * NH + h + 1
                        b = h % 2
                        if s == QK_AT[h] + PT_LAG:
                            pe.wait_ge(P_ready, n)
                            if h >= 1:
                                pe.wait_ge(PT_out, n - 1)
                            for kt in range(MT):
                                for t in range(MT):
                                    i = nc.tensor.transpose(M[2][:, kt * SEQ + t * P:kt * SEQ + (t + 1) * P],
                                                            prob[:, b, t, kt * P:(kt + 1) * P], ident[:, :])
                            i.then_inc(PT_done, 1)
                    for h in range(NH):
                        n = l * NH + h + 1
                        b = h % 2
                        mem_head = h - HEADS
                        if s == QK_AT[h]:
                            if h == 0:
                                pe.wait_ge(acc_act, l * READS_ACT + 13 + ACC_CREDIT)
                                pe.wait_ge(rope_out, l * 5 + 5)
                                pe.wait_ge(lat[1]["lo"], l + 1)
                            if h == HEADS:
                                pe.wait_ge(acc_act, l * READS_ACT + 14 + ACC_CREDIT)
                            if h >= 2:
                                pe.wait_ge(exp_ready, n - 2)
                            for t in range(MT):
                                tok = slice(t * P, (t + 1) * P)
                                o = M[b][:, t * SEQ:(t + 1) * SEQ]
                                if h < HEADS:
                                    pb = 64 * (h % 2)
                                    mm(o, O[:, h, tok], kn[:, h, :], True, False)
                                    i = mm(o, qpe[pb:pb + 64, h // 2, tok], kpe[pb:pb + 64, :], False, True)
                                else:
                                    i = mm(o, O[:, h + CT, tok], mkT[:, mem_head, :], True, True)
                            i.then_inc(S_ready, 1)
                    if s + 1 in MOD_T_AT:
                        c = MOD_T_AT.index(s + 1)
                        pe.wait_ge(mod_used, l * MU + 8 * c + 8 + MRING)
                        if c >= 1:
                            pe.wait_ge(mod_out, l * MCH + c)
                        if LAT_AT[1] + ROW_LAG <= s < QK_AT[0] + PV_LAG:
                            pe.wait_ge(lat[1]["val"], l + 1)
                        heads = sum(q + PV_LAG <= s for q in QK_AT)
                        if heads:
                            pe.wait_ge(o_out, l * NH + heads)
                        for t in range(4):
                            i = mm(M[3][:, MODCOL + t:MODCOL + t + 1], modacc[:, c % 2, t * P:(t + 1) * P], ones[:, 0:1], True, True)
                        i.then_inc(mod_T, 1)
                    if s == LH:
                        continue
                    g = group_of(s)
                    name, kind, width, units, nk = GROUPS[g]
                    first, last = s == H_AT[g], s == H_AT[g + 1] - 1
                    n = nk // 2
                    k0 = (s - H_AT[g]) * n
                    if name == "mem":
                        j, v = s // 4, s // 2 % 2
                        if s in (0, 2):
                            pe.wait_ge(acc_act, l * READS_ACT + v - 1 + ACC_CREDIT)
                            pe.wait_ge(acc_dve, l * READS_DVE + v - 1 + ACC_CREDIT)
                        k0 = 4 * j + s % 2 * n
                        pe.wait_ge(mem_lo, l * KT + k0 + n)
                        wait_lo(s)
                        product = tm_half if v else fm_half
                        args = (s, acc[v], (memh, meml)) + (() if v else (four,)) + (k0 % 8, n, k0 == 0, k0 + n == KT, width)
                        product(*args).then_inc(half_used, 1)
                        continue
                    if first:
                        pe.wait_ge(acc_act, l * READS_ACT + (g if g < 3 else sum(r <= g - 2 for r in ACT_READS)) + ACC_CREDIT)
                        if g - 2 in DVE_READS:
                            pe.wait_ge(acc_dve, l * READS_DVE + sum(r <= g - 2 for r in DVE_READS) + ACC_CREDIT)
                    if name == "qlat":
                        pe.wait_ge(x_lo, l * KT + k0 + n)
                    if name == "uq" and first:
                        pe.wait_ge(lat[0]["lo"], l + 1)
                    if name == "ukv" and first:
                        pe.wait_ge(lat[1]["lo"], l + 1)
                    if name == "wo":
                        pe.wait_ge(y_lo, l * 4 + GATE_PART.index(k0 // 4) + 1)
                    wait_lo(s)
                    act_in = (Yhi, Ylo) if name == "wo" else (Hhi, Hlo)
                    a = acc[acc_of(g)]
                    if kind == "FM":
                        w = fm_half(s, a, act_in, four[0:width // P], k0, n, first, last, width)
                    elif kind == "TM":
                        w = tm_half(s, a, act_in, k0, n, first, last, width)
                    elif kind == "UQ":
                        w = fm_half(s, a, (qlh, qll), four[0:3], k0, n, first, last, width)
                    else:
                        w = ukv_half(s, a, k0, first, last)
                    w.then_inc(half_used, 1)
            pe.wait_ge(r_ready, 1)
            nc.tensor.transpose(M[0][0:2 * KT, 0:P], R[:, :], ident[:, :]).then_inc(r_T, 1)
            even, odd = slice(0, P + 1), slice(P + 1, SEQ)
            pe.wait_ge(acc_dve, DVE0)
            pe.wait_ge(rows_ready, 1)
            for t in range(MT):
                pe.wait_ge(csx_ready, t + 1)
                for g in range(KT // 2):
                    for j in range(2):
                        f = 2 * g + j
                        o = bank(g)[:, j * SEQ:(j + 1) * SEQ]
                        rows_in = X[:, t, f * P:(f + 1) * P]
                        mm(o[:, even], rows_in, csx[:, t, 0:P + 1], j == 0 and t == 0, False)
                        i = mm(o[:, odd], rows_in, csx[:, t, SEQ + 1:SEQ + P], False, t == MT - 1)
                    if t == MT - 1:
                        i.then_inc(ab_ps, 1)
            for g in range(KT // 2):
                pe.wait_ge(ab_val, g + 1)
                for j in range(2):
                    o = bank(g)[:, j * SEQ:(j + 1) * SEQ]
                    for i in range(2):
                        mm(o[:, even], cs[:, i, j * P:(j + 1) * P], AB[:, 2 * g + i, even], j == 0 and i == 0, False)
                        w = mm(o[:, odd], cs[:, i, SEQ + j * P:SEQ + (j + 1) * P], AB[:, 2 * g + i, odd], False, i == 1)
                w.then_inc(f_ps, 1)
            for s in range(32):
                n = s // 8
                if s % 8 == 0:
                    if n < 2:
                        pe.wait_ge(f_pq, 2 * n + 2)
                    else:
                        pe.wait_ge(acc_act, ACT0 + n - 1)
                        pe.wait_ge(acc_dve, DVE0 + n - 1)
                pe.wait_ge(f_lo, min(s + 1, KT // 2))
                pe.wait_ge(lo_ready, LO0 + s + 1)
                tm_half(s, acc[n % 2], (Hhi, Hlo), 2 * (s % 8), 2, s % 8 == 0, s % 8 == 7, 512).then_inc(half_used, 1)
            def x2_tile(f, t):
                return nc.tensor.transpose(bank(f // 2)[:, f % 2 * SEQ + t * P:f % 2 * SEQ + (t + 1) * P],
                                           X[:, t, f * P:(f + 1) * P], ident[:, :])

            for t in range(MT):
                pe.wait_ge(x_new, 2 * (DEPTH + 1) + t + 1)
                for f in range(KT - 1):
                    w = x2_tile(f, t)
            w.then_inc(x2_T, 1)
            pe.wait_ge(x2_rot, 1)
            for t in range(MT):
                w = nc.tensor.transpose(M[3][:, SEQ + t * P:SEQ + (t + 1) * P], xrot[:, t, :], ident[:, :])
            w.then_inc(x2_row, 1)
            pe.wait_ge(x2_rowed, 1)
            for t in range(MT):
                w = x2_tile(KT - 1, t)
            w.then_inc(x2_T, 1)
            with pe.Fori(0, 4) as q:
                base = ML_H + 64 * q
                for s in range(64):
                    n = s // 8
                    if s % 8 == 0 and n < 2:
                        pe.wait_ge(x2_val, 4 * n + 4)
                        pe.wait_ge(acc_dve, DVE1 + 4 * q + n - 1)
                    if s % 8 == 0 and 2 <= n < 6:
                        pe.wait_ge(m_rel, 4 * q + n - 1)
                    if s % 8 == 0 and n >= 6:
                        pe.wait_ge(acc_dve, DVE1 + 4 * q + n - 5)
                    if n < 1:
                        pe.wait_ge(x2_lo, s + 1)
                        pe.wait_ge(x2_lo_pool, s + 1)
                    if n == 4:
                        pe.wait_ge(m_lo, 4 * q + (s - 32) // 2 + 1)
                    pe.wait_ge(lo_ready, LO0 + 32 + 64 * q + s + 1)
                    k0 = 2 * (s % 8)
                    if n < 4:
                        w = fm_half(s, acc[n % 2], (Hhi, Hlo), four, k0, 2, k0 == 0, k0 == 14, 512)
                    else:
                        w = tm_half(s, acc[n % 2], (Yhi, Ylo), k0, 2, k0 == 0, k0 == 14, 512)
                    w.then_inc(half_used, 1)


def kernel(**inputs):
    import numpy as np
    import concourse.bacc as bacc
    from concourse.bass_utils import run_bass_kernel_spmd

    a = {k: np.asarray(v) for k, v in inputs.items()}

    def fm(v):
        return np.ascontiguousarray(np.moveaxis(v.reshape(*v.shape[:-1], -1, P), -1, -2))

    pad = np.zeros((DEPTH, P, G_CONST - C_CONV - 3 * CT), np.float32)
    conv = np.moveaxis(a["conv_w"].reshape(DEPTH, 3, CT, P), (1, 2, 3), (3, 2, 1)).reshape(DEPTH, P, 3 * CT)
    small = np.concatenate([fm(a["pre_norm_g"]), fm(a["mem_norm_g"]), fm(a["q_norm_g"]), fm(a["kv_norm_g"]), conv, pad], axis=2)
    small = np.concatenate([small, small[-1:]])
    half = ROPE // 2
    freq = np.float32(1.0) / (10000.0 ** (np.arange(0, ROPE, 2) / ROPE)).astype(np.float32)
    sign = np.tile(np.repeat(np.array([-1.0, 1.0], np.float32), half), 2)
    rope_c = np.stack([np.tile(freq, P // half), sign], axis=1).astype(np.float32)
    turn = 2.0 * np.pi * (np.outer(np.arange(SEQ), np.arange(SEQ)) % SEQ) / SEQ
    dft = np.concatenate([np.cos(turn), np.sin(turn)], axis=1).astype(np.float32)
    uq = a["w_uq"].reshape(DEPTH, QL, HEADS // 2, 2, QHEAD)
    uq = np.concatenate([uq[..., :NOPE].reshape(DEPTH, QL, HEADS // 2, 2 * NOPE),
                         uq[..., NOPE:].reshape(DEPTH, QL, HEADS // 2, 2 * ROPE)], axis=3).reshape(DEPTH, QL, HEADS * QHEAD)
    arrays = {
        "x": a["x"][0], "memt": a["mem"][0].T.reshape(KT, P, SEQ),
        "positions": a["positions"].reshape(SEQ), "small": np.ascontiguousarray(small),
        "w_in": a["w_in"], "w_uq": uq, "w_ukv": a["w_ukv"], "w_mk": a["w_mk"], "w_mv": a["w_mv"], "w_o": a["w_o"],
        "post_g": a["post_norm_g"], "consts": np.eye(P, dtype=np.float32), "rope_c": rope_c, "dft": dft,
        "cvec": fm(a["c_2"][0]), "bmod": fm(a["b_mod_2"][0]),
        "ng2": np.ascontiguousarray(np.moveaxis(fm(a["norm_g_2"][0]), 0, 1).reshape(P, 4 * KT)),
        "w_mod": a["w_mod_2"][0], "w_fnet": a["fnet_w_out_2"][0], "w_mlp_in": a["w_mlp_in_2"][0], "w_mlp_out": a["w_mlp_out_2"][0],
    }
    arrays = {k: np.ascontiguousarray(v) for k, v in arrays.items()}
    nc = bacc.Bacc("TRN2", target_bir_lowering=False, num_devices=1)
    aps = {k: nc.dram_tensor(f"in_{k}", v.shape, mybir.dt.from_np(v.dtype), kind="ExternalInput").ap() for k, v in arrays.items()}
    out = nc.dram_tensor("out_0", [SEQ, D], F32, kind="ExternalOutput").ap()
    build_program(nc, **aps, out=out)
    r = run_bass_kernel_spmd(nc, [{f"in_{k}": v for k, v in arrays.items()}], core_ids=[0])
    return r.results[0]["out_0"].reshape(1, SEQ, D)
```
